# Optimizing a Trainium2 kernel written in Bass

```python
import math
import jax, jax.numpy as jnp
from jax import lax
import numpy as np

D_MODEL = 1024
BATCH = 1
SEQ = 256
DEPTH = 1

N_HEADS = 8
HEAD_DIM = D_MODEL // (2 * N_HEADS)
V_DIM = 2 * HEAD_DIM
ATTN_WIDTH = N_HEADS * V_DIM
CONV_CH = D_MODEL
CONV_WIDTH = 31
FF_DIM = ((8 * D_MODEL // 3 + 255) // 256) * 256
NUM_BUCKETS = 32
MAX_DISTANCE = 128
Q_BLOCK = 128
EPS = 1e-6

Q_COLS = N_HEADS * 2 * HEAD_DIM
K_COLS = N_HEADS * 2 * HEAD_DIM
V_COLS = N_HEADS * V_DIM
U_COLS = 2 * CONV_CH
G_COLS = 2 * D_MODEL
IN_COLS = Q_COLS + K_COLS + V_COLS + U_COLS + G_COLS


def rms_norm(x, w):
    xf = x.astype(jnp.float32)
    y = xf * lax.rsqrt(jnp.mean(xf * xf, axis=-1, keepdims=True) + EPS)
    return (y * w.astype(jnp.float32)).astype(x.dtype)

def layer_norm(x, w, b):
    xf = x.astype(jnp.float32)
    mu = jnp.mean(xf, axis=-1, keepdims=True)
    xc = xf - mu
    var = jnp.mean(xc * xc, axis=-1, keepdims=True)
    y = xc * lax.rsqrt(var + EPS) * w.astype(jnp.float32) + b.astype(jnp.float32)
    return y.astype(x.dtype)

def t5_bucket(rel):
    n = jnp.maximum(rel, 0)
    max_exact = NUM_BUCKETS // 2
    nf = jnp.maximum(n, 1).astype(jnp.float32)
    large = max_exact + (jnp.log(nf / max_exact) / math.log(MAX_DISTANCE / max_exact)
                         * (NUM_BUCKETS - max_exact)).astype(jnp.int32)
    large = jnp.minimum(large, NUM_BUCKETS - 1)
    return jnp.where(n < max_exact, n, large)

def diff_attention(q1, q2, k1, k2, v, lam, rel_bias):
    B, H, S, _ = q1.shape
    nb = S // Q_BLOCK
    scale = HEAD_DIM ** -0.5
    f32 = jnp.float32
    k1f, k2f, vf = k1.astype(f32), k2.astype(f32), v.astype(f32)
    lamf = lam.astype(f32)
    k_pos = jnp.arange(S, dtype=jnp.int32)
    bias_tab = rel_bias.astype(f32)

    def block(i):
        start = i * Q_BLOCK
        qb1 = lax.dynamic_slice_in_dim(q1, start, Q_BLOCK, axis=2).astype(f32)
        qb2 = lax.dynamic_slice_in_dim(q2, start, Q_BLOCK, axis=2).astype(f32)
        q_pos = start + jnp.arange(Q_BLOCK, dtype=jnp.int32)
        rel = q_pos[:, None] - k_pos[None, :]
        bias = jnp.transpose(bias_tab[t5_bucket(rel)], (2, 0, 1))
        causal = rel >= 0

        def probs(qb, kf):
            s = jnp.einsum('bhqd,bhkd->bhqk', qb, kf) * scale + bias
            s = jnp.where(causal, s, -jnp.inf)
            return jax.nn.softmax(s, axis=-1)

        p = probs(qb1, k1f) - lamf * probs(qb2, k2f)
        return jnp.einsum('bhqk,bhkd->bhqd', p, vf)

    out = lax.map(block, jnp.arange(nb))
    out = jnp.transpose(out, (1, 0, 3, 2, 4)).reshape(B, S, H, V_DIM)
    return out.astype(q1.dtype)

def causal_depthwise_conv(u, w, b):
    up = jnp.pad(u, ((0, 0), (CONV_WIDTH - 1, 0), (0, 0)))
    y = lax.conv_general_dilated(up, w[:, None, :], window_strides=(1,), padding='VALID',
                                 dimension_numbers=('NWC', 'WIO', 'NWC'),
                                 feature_group_count=CONV_CH)
    return y + b

def first_inputs(seed: int = 0) -> dict:
    key = jax.random.key(seed)
    ks = jax.random.split(key, 24)
    n = jax.random.normal
    f = jnp.float32

    def gain(k, shape):
        return 1.0 + 0.05 * n(k, shape, f)

    return {
        "x": n(ks[0], (BATCH, SEQ, D_MODEL), f),
        "attn_norm_w": gain(ks[1], (DEPTH, D_MODEL)),
        "w_in": n(ks[2], (DEPTH, D_MODEL, IN_COLS), f) * D_MODEL ** -0.5,
        "q_norm_w": gain(ks[3], (DEPTH, HEAD_DIM)),
        "k_norm_w": gain(ks[4], (DEPTH, HEAD_DIM)),
        "lam_q1": 0.1 * n(ks[5], (DEPTH, HEAD_DIM), f),
        "lam_k1": 0.1 * n(ks[6], (DEPTH, HEAD_DIM), f),
        "lam_q2": 0.1 * n(ks[7], (DEPTH, HEAD_DIM), f),
        "lam_k2": 0.1 * n(ks[8], (DEPTH, HEAD_DIM), f),
        "subln_w": gain(ks[9], (DEPTH, V_DIM)),
        "w_proj_attn": n(ks[10], (DEPTH, ATTN_WIDTH, D_MODEL), f) * ATTN_WIDTH ** -0.5,
        "conv_w": n(ks[11], (DEPTH, CONV_WIDTH, CONV_CH), f) * CONV_WIDTH ** -0.5,
        "conv_b": 0.02 * n(ks[12], (DEPTH, CONV_CH), f),
        "conv_ln_w": gain(ks[13], (DEPTH, CONV_CH)),
        "conv_ln_b": 0.02 * n(ks[14], (DEPTH, CONV_CH), f),
        "w_proj_conv": n(ks[15], (DEPTH, CONV_CH, D_MODEL), f) * CONV_CH ** -0.5,
        "gate_b": 0.02 * n(ks[16], (DEPTH, G_COLS), f),
        "w_out": n(ks[17], (DEPTH, D_MODEL, D_MODEL), f) * D_MODEL ** -0.5,
        "ffn_norm_w": gain(ks[18], (DEPTH, D_MODEL)),
        "w_gate_up": n(ks[19], (DEPTH, D_MODEL, 2 * FF_DIM), f) * D_MODEL ** -0.5,
        "w_down": n(ks[20], (DEPTH, FF_DIM, D_MODEL), f) * FF_DIM ** -0.5,
        "rel_bias": 0.5 * n(ks[21], (NUM_BUCKETS, N_HEADS), f),
    }

def first_block(x, attn_norm_w, w_in, q_norm_w, k_norm_w, lam_q1, lam_k1, lam_q2, lam_k2,
              subln_w, w_proj_attn, conv_w, conv_b, conv_ln_w, conv_ln_b, w_proj_conv,
              gate_b, w_out, ffn_norm_w, w_gate_up, w_down, rel_bias):
    B, S, _ = x.shape
    splits = np.cumsum([Q_COLS, K_COLS, V_COLS, U_COLS]).tolist()
    for l in range(DEPTH):
        lam_init = 0.8 - 0.6 * math.exp(-0.3 * l)
        h = rms_norm(x, attn_norm_w[l])
        proj = h @ w_in[l]
        q, k, v, u, g = jnp.split(proj, splits, axis=-1)

        q = rms_norm(q.reshape(B, S, N_HEADS, 2, HEAD_DIM), q_norm_w[l])
        k = rms_norm(k.reshape(B, S, N_HEADS, 2, HEAD_DIM), k_norm_w[l])
        q = jnp.transpose(q, (3, 0, 2, 1, 4))
        k = jnp.transpose(k, (3, 0, 2, 1, 4))
        v = jnp.transpose(v.reshape(B, S, N_HEADS, V_DIM), (0, 2, 1, 3))
        lam = (jnp.exp(jnp.sum(lam_q1[l].astype(jnp.float32) * lam_k1[l].astype(jnp.float32)))
               - jnp.exp(jnp.sum(lam_q2[l].astype(jnp.float32) * lam_k2[l].astype(jnp.float32)))
               + lam_init)
        a = diff_attention(q[0], q[1], k[0], k[1], v, lam, rel_bias)
        a = rms_norm(a, subln_w[l]) * (1.0 - lam_init)
        y_a = a.reshape(B, S, ATTN_WIDTH) @ w_proj_attn[l]

        u_a, u_b = jnp.split(u, 2, axis=-1)
        c = causal_depthwise_conv(u_a * jax.nn.sigmoid(u_b), conv_w[l], conv_b[l])
        c = jax.nn.silu(layer_norm(c, conv_ln_w[l], conv_ln_b[l]))
        y_b = c @ w_proj_conv[l]

        g_a, g_b = jnp.split(jax.nn.sigmoid(g + gate_b[l]), 2, axis=-1)
        x = x + (g_a * y_a + g_b * y_b) @ w_out[l]

        h = rms_norm(x, ffn_norm_w[l])
        gt, up = jnp.split(h @ w_gate_up[l], 2, axis=-1)
        x = x + (jax.nn.silu(gt) * up) @ w_down[l]
    return x


HEAD_DIM_2 = 64
N_ATTN_HEADS = 8
ATTN_WIDTH_2 = N_ATTN_HEADS * HEAD_DIM_2
LRU_WIDTH = D_MODEL - ATTN_WIDTH_2
N_LRU_BLOCKS = 8
LRU_BLOCK = LRU_WIDTH // N_LRU_BLOCKS
MIX_WIDTH = ATTN_WIDTH_2 + LRU_WIDTH
IN_WIDTH = 3 * ATTN_WIDTH_2 + 2 * LRU_WIDTH
CONV_WIDTH_2 = 4
LRU_C = 8.0
D_FF = 4 * D_MODEL
BLOCK_Q = 128


def rms_norm_2(x, g):
    xf = x.astype(jnp.float32)
    y = xf * lax.rsqrt(jnp.mean(xf * xf, axis=-1, keepdims=True) + EPS)
    return (y * g.astype(jnp.float32)).astype(x.dtype)

def causal_depthwise_conv_2(u, w, b):
    S = u.shape[1]
    up = jnp.pad(u, ((0, 0), (CONV_WIDTH_2 - 1, 0), (0, 0)))
    out = b
    for k in range(CONV_WIDTH_2):
        out = out + up[:, k:k + S] * w[k]
    return out

def _linear_rec_combine(left, right):
    a1, b1 = left
    a2, b2 = right
    return a1 * a2, a2 * b1 + b2

def rg_lru(u, w_rg, b_rg, w_ig, b_ig, lam):
    B, S, _ = u.shape
    ub = u.reshape(B, S, N_LRU_BLOCKS, LRU_BLOCK)
    r = jax.nn.sigmoid(jnp.einsum('bsnc,ncd->bsnd', ub, w_rg) + b_rg.reshape(N_LRU_BLOCKS, LRU_BLOCK))
    i = jax.nn.sigmoid(jnp.einsum('bsnc,ncd->bsnd', ub, w_ig) + b_ig.reshape(N_LRU_BLOCKS, LRU_BLOCK))
    r = r.reshape(B, S, LRU_WIDTH).astype(jnp.float32)
    i = i.reshape(B, S, LRU_WIDTH).astype(jnp.float32)
    log_a = -LRU_C * r * jax.nn.softplus(-lam.astype(jnp.float32))
    a = jnp.exp(log_a)
    mult = jnp.sqrt(-jnp.expm1(2.0 * log_a))
    bterm = mult * (i * u.astype(jnp.float32))
    _, h = lax.associative_scan(_linear_rec_combine, (a, bterm), axis=1)
    return h.astype(u.dtype)

def stick_breaking_attention(q, k, v):
    S = q.shape[1]
    scale = 1.0 / math.sqrt(HEAD_DIM_2)
    qf = q.astype(jnp.float32)
    kf = k.astype(jnp.float32)
    vf = v.astype(jnp.float32)
    outs = []
    for blk in range(S // BLOCK_Q):
        q0 = blk * BLOCK_Q
        end = q0 + BLOCK_Q
        z = jnp.einsum('bqhd,bkhd->bhqk', qf[:, q0:end], kf[:, :end]) * scale
        qpos = q0 + jnp.arange(BLOCK_Q)[:, None]
        kpos = jnp.arange(end)[None, :]
        mask = kpos < qpos
        log_one_minus = jnp.where(mask, jax.nn.log_sigmoid(-z), 0.0)
        suffix = lax.cumsum(log_one_minus, axis=3, reverse=True) - log_one_minus
        log_w = jax.nn.log_sigmoid(z) + suffix
        w = jnp.where(mask, jnp.exp(log_w), 0.0)
        outs.append(jnp.einsum('bhqk,bkhd->bqhd', w, vf[:, :end]))
    return jnp.concatenate(outs, axis=1).astype(v.dtype)

def hybrid_mixer(h, w_in, conv_w, conv_b, w_rg, b_rg, w_ig, b_ig, lam, q_norm_g, k_norm_g, w_out):
    B, S, _ = h.shape
    proj = h @ w_in
    q, k, v, xl, gl = jnp.split(proj, [ATTN_WIDTH_2, 2 * ATTN_WIDTH_2, 3 * ATTN_WIDTH_2, 3 * ATTN_WIDTH_2 + LRU_WIDTH], axis=-1)
    q = rms_norm_2(q.reshape(B, S, N_ATTN_HEADS, HEAD_DIM_2), q_norm_g)
    k = rms_norm_2(k.reshape(B, S, N_ATTN_HEADS, HEAD_DIM_2), k_norm_g)
    v = v.reshape(B, S, N_ATTN_HEADS, HEAD_DIM_2)
    attn = stick_breaking_attention(q, k, v).reshape(B, S, ATTN_WIDTH_2)
    xl = causal_depthwise_conv_2(xl, conv_w, conv_b)
    lru = rg_lru(xl, w_rg, b_rg, w_ig, b_ig, lam) * jax.nn.gelu(gl)
    return jnp.concatenate([attn, lru], axis=-1) @ w_out

def sq_relu_mlp(h, w_up, w_down):
    return jnp.square(jax.nn.relu(h @ w_up)) @ w_down

def second_inputs(seed: int = 0) -> dict:
    key = jax.random.key(seed)
    ks = jax.random.split(key, 17)
    f32 = jnp.float32
    nrm = lambda kk, shape, s: jax.random.normal(kk, shape, f32) * s
    a0 = jax.random.uniform(ks[10], (DEPTH, LRU_WIDTH), f32, minval=0.9, maxval=0.999)
    return {
        'x': jax.random.normal(ks[0], (BATCH, SEQ, D_MODEL), f32),
        'norm1_g': 1.0 + nrm(ks[1], (DEPTH, D_MODEL), 0.02),
        'w_in': nrm(ks[2], (DEPTH, D_MODEL, IN_WIDTH), D_MODEL ** -0.5),
        'conv_w': nrm(ks[3], (DEPTH, CONV_WIDTH_2, LRU_WIDTH), CONV_WIDTH_2 ** -0.5),
        'conv_b': nrm(ks[4], (DEPTH, LRU_WIDTH), 0.01),
        'w_rg': nrm(ks[5], (DEPTH, N_LRU_BLOCKS, LRU_BLOCK, LRU_BLOCK), LRU_BLOCK ** -0.5),
        'b_rg': nrm(ks[6], (DEPTH, LRU_WIDTH), 0.01),
        'w_ig': nrm(ks[7], (DEPTH, N_LRU_BLOCKS, LRU_BLOCK, LRU_BLOCK), LRU_BLOCK ** -0.5),
        'b_ig': nrm(ks[8], (DEPTH, LRU_WIDTH), 0.01),
        'lru_lambda': jnp.log(a0) - jnp.log1p(-a0),
        'q_norm_g': 1.0 + nrm(ks[11], (DEPTH, HEAD_DIM_2), 0.02),
        'k_norm_g': 1.0 + nrm(ks[12], (DEPTH, HEAD_DIM_2), 0.02),
        'w_out': nrm(ks[13], (DEPTH, MIX_WIDTH, D_MODEL), MIX_WIDTH ** -0.5),
        'norm2_g': 1.0 + nrm(ks[14], (DEPTH, D_MODEL), 0.02),
        'w_up': nrm(ks[15], (DEPTH, D_MODEL, D_FF), D_MODEL ** -0.5),
        'w_down': nrm(ks[16], (DEPTH, D_FF, D_MODEL), D_FF ** -0.5),
    }

def second_block(x, norm1_g, w_in, conv_w, conv_b, w_rg, b_rg, w_ig, b_ig, lru_lambda, q_norm_g, k_norm_g, w_out, norm2_g, w_up, w_down):
    for l in range(DEPTH):
        h = rms_norm_2(x, norm1_g[l])
        x = x + hybrid_mixer(h, w_in[l], conv_w[l], conv_b[l], w_rg[l], b_rg[l], w_ig[l], b_ig[l],
                             lru_lambda[l], q_norm_g[l], k_norm_g[l], w_out[l])
        h = rms_norm_2(x, norm2_g[l])
        x = x + sq_relu_mlp(h, w_up[l], w_down[l])
    return x


def setup_inputs(seed=0):
    out = dict(first_inputs(seed))
    for name, value in second_inputs(seed + 1).items():
        if name != "x":
            out[name + "_2"] = value
    return out


def reference(
    x, attn_norm_w, w_in, q_norm_w, k_norm_w, lam_q1, lam_k1, lam_q2, lam_k2, subln_w,
    w_proj_attn, conv_w, conv_b, conv_ln_w, conv_ln_b, w_proj_conv, gate_b, w_out, ffn_norm_w,
    w_gate_up, w_down, rel_bias, norm1_g_2, w_in_2, conv_w_2, conv_b_2, w_rg_2, b_rg_2, w_ig_2,
    b_ig_2, lru_lambda_2, q_norm_g_2, k_norm_g_2, w_out_2, norm2_g_2, w_up_2, w_down_2,
):
    x = first_block(
        x, attn_norm_w, w_in, q_norm_w, k_norm_w, lam_q1, lam_k1, lam_q2, lam_k2, subln_w,
        w_proj_attn, conv_w, conv_b, conv_ln_w, conv_ln_b, w_proj_conv, gate_b, w_out,
        ffn_norm_w, w_gate_up, w_down, rel_bias,
    )
    return second_block(
        x, norm1_g_2, w_in_2, conv_w_2, conv_b_2, w_rg_2, b_rg_2, w_ig_2, b_ig_2, lru_lambda_2,
        q_norm_g_2, k_norm_g_2, w_out_2, norm2_g_2, w_up_2, w_down_2,
    )


_drawn_inputs = setup_inputs


def setup_inputs(seed=0):
    import zlib

    import numpy as np

    out = dict(_drawn_inputs(seed))
    spreads = {}
    factors = {'lam_q1': 64.0,
     'lam_k2': 2.951,
     'conv_b': 3.47,
     'conv_ln_b': 7.077,
     'gate_b': 8.0,
     'norm1_g_2': 5.114,
     'conv_b_2': 7.828,
     'b_rg_2': 42.155,
     'b_ig_2': 33.424,
     'q_norm_g_2': 8.0,
     'k_norm_g_2': 8.0,
     'norm2_g_2': 10.733}
    for name, (base, spread) in spreads.items():
        noise = np.random.default_rng([zlib.crc32(name.encode()), seed]).standard_normal(out[name].shape)
        drawn = base * np.exp(spread * noise) if base else spread * noise
        out[name] = __import__('jax').numpy.asarray(drawn.astype(out[name].dtype))
    for name, factor in factors.items():
        out[name] = (out[name] * factor).astype(out[name].dtype)
    return out
```

```python
import math
from contextlib import ExitStack

import numpy as np

import concourse.bass as bass
from concourse import mybir

F32 = mybir.dt.float32
F32R = mybir.dt.float32r
ALU = mybir.AluOpType
ACT = mybir.ActivationFunctionType
AX = mybir.AxisListType

P = 128
D = 1024
S = 256
NT = S // P
EPS = 1e-6
KT = D // P
CW = 512
UK = 4

H = 8
HD = 64
SC = HD ** -0.5
TAPS = 31
PAD = TAPS - 1
FF = 2816
FK = FF // P
BUCKETS, MAX_DIST = 32, 128
MASKED = -1e30
LAM_INIT = 0.8 - 0.6 * math.exp(-0.3 * 0)
RELS = 384

W2 = 512
CT2 = W2 // P
IN2 = 3 * W2 + 2 * W2
TAPS2 = 4
FF2 = 4 * D
FK2 = FF2 // P
LRU_C = 8.0
EXP_LN_TABLES = 6
ZC = 384

R_CONV_W, R_CONV_B, R_LN_W, R_LN_B = 0, 31, 32, 33
R_NORM = (34, 35, 36, 37)
R_CONV2_W, R_CONV2_B, R_RG, R_IG, R_LAMBDA = 38, 42, 43, 44, 45
R_Q, R_K, R_SUB, R_Q2, R_K2 = 46, 47, 48, 49, 50
VROWS = 64


def weight_chunks(w):
    half = [0, UK]
    q = lambda g: ("q", g, w["w_in"], CW * g, None, half, KT)
    k = lambda g: ("k", g, w["w_in"], D + CW * g, None, half, KT)
    v = lambda g: ("v", g, w["w_in"], 2 * D + CW * g, None, half, KT)
    u = lambda i: ("u", i, w["w_in"], 3 * D + 256 * i, D, half, KT)
    out = [u(0), q(0), k(0), u(1), v(0), q(1), k(1), u(2), v(1), u(3)]
    out += [("g", i, w["w_in"], 5 * D + CW * i, None, half, KT) for i in range(4)]
    out += [("pa", i, w["w_proj_attn"], CW * i, None, half, KT) for i in range(2)]
    out += [("pc", i, w["w_proj_conv"], CW * i, None, half, KT) for i in range(2)]
    out += [("res", i, w["w_out"], CW * i, None, half, KT) for i in range(2)]
    out += [("ff", i, w["w_gate_up"], 256 * i, FF, half, KT) for i in range(FF // 256)]
    out += [("res", 2 + i, w["w_down"], CW * i, None, list(range(0, FK, UK)), FK) for i in range(2)]
    out += [("x2", 0, w["w_in_2"], 3 * W2, None, half, KT), ("q", 2, w["w_in_2"], 0, None, half, KT),
            ("k", 2, w["w_in_2"], W2, None, half, KT), ("g2", 0, w["w_in_2"], 4 * W2, None, half, KT),
            ("v", 2, w["w_in_2"], 2 * W2, None, half, KT)]
    out += [("res", 4 + i, w["w_out_2"], CW * i, None, [UK, 0], KT) for i in range(2)]
    out += [("up", i, w["w_up_2"], CW * i, None, half, KT) for i in range(FF2 // CW)]
    out += [("res", 6 + i, w["w_down_2"], CW * i, None, list(range(0, FK2, UK)), FK2) for i in range(2)]
    return out


def build(nc, a, out):
    chunks = weight_chunks(a)
    units = []
    for c, ch in enumerate(chunks):
        for n, k0 in enumerate(ch[5]):
            units.append((c, k0, min(UK, ch[6] - k0), n == 0, n == len(ch[5]) - 1))
    u0 = next(u for u, x in enumerate(units) if chunks[x[0]][:2] == ("res", 4))
    units[u0 + 1], units[u0 + 2] = units[u0 + 2], units[u0 + 1]
    first = [next(u for u, x in enumerate(units) if x[0] == c) for c in range(len(chunks))]
    last = [max(u for u, x in enumerate(units) if x[0] == c) for c in range(len(chunks))]
    NU = len(units)
    number = {(ch[0], ch[1]): c for c, ch in enumerate(chunks)}
    end = {key: last[c] + 1 for key, c in number.items()}
    begin = {key: first[c] for key, c in number.items()}
    STAGE = [0, 1, 2, 0]
    ended = {last[c] + 1: (chunks[c][0], chunks[c][1], c) for c in range(len(chunks))}

    RAW, SPLIT = 3, 3
    LEAD = 2

    raw_value = []
    for u, (c, *_) in enumerate(units):
        raw_value.append((raw_value[u - RAW] if u >= RAW else 0) + (16 if chunks[c][4] is None else 32))

    def on_pool(u):
        return 5 <= u <= 31
    low_no = []
    counts = {True: 0, False: 0}
    for u in range(NU):
        counts[on_pool(u)] += 1
        low_no.append(counts[on_pool(u)])

    ATT = [*range(8, 24)]
    NA = 2 * H
    CONV_OPS = TAPS * KT
    quota = {}
    done_ops = 0
    avail = {}
    for i in range(4):
        avail[i] = end["u", i] + 2
    for s in range(NU + 1):
        n = 11 if s < 24 else 14
        pairs = sum(1 for i in range(4) if avail[i] <= s)
        quota[s] = max(0, min(n, 2 * TAPS * pairs - done_ops))
        done_ops += quota[s]
    conv_last = max(s for s in range(NU) if quota[s])
    LN = conv_last
    B = begin["x2", 0]

    with ExitStack() as ctx:
        cursor = [(nc.sbuf_base + 31) // 32 * 32]

        def place(name, shape, dt=F32, at=None):
            size = int(np.prod(shape[1:])) * 4
            if at is None:
                at = cursor[0]
                cursor[0] += (size + 31) // 32 * 32
            return nc.alloc_sbuf_tensor_at(name, shape, dt, offset=at), at

        def sb(name, shape, dt=F32, at=None):
            return place(name, shape, dt, at)[0]

        def sem(name):
            return ctx.enter_context(nc.semaphore(name))

        raw = sb("raw", [P, RAW, UK, CW])
        w_hi = sb("w_hi", [P, SPLIT, UK, CW], F32R)
        w_lo = sb("w_lo", [P, SPLIT, UK, CW], F32R)
        h_hi = sb("h_hi", [P, KT, S], F32R)
        h_lo, at = place("h_lo", [P, KT, S], F32R)
        c_sq = sb("c_sq", [P, KT, S], at=at)
        c_hi = sb("c_hi", [P, KT, S], F32R)
        c_lo = sb("c_lo", [P, KT, S], F32R)
        conv, at = place("conv", [P, KT, S])
        x_res = sb("x_res", [P, NT, D], at=at)
        vec_t = sb("vec_t", [P, KT, VROWS])
        ident = sb("ident", [P, P])
        mean_w = sb("mean_w", [P, P])
        rstd = sb("rstd", [P, 4, NT])
        ss = sb("ss", [P, 4, 2, NT])
        ms = sb("ms", [P, 4, NT])
        nhalf = sb("nhalf", [P, 16])
        small = sb("small", [P, 64])
        qk_ss = sb("qk_ss", [P, 16])
        qk_r = sb("qk_r", [P, 16])
        lam_v = sb("lam_v", [P, 4, HD])
        gains = sb("gains", [P, 4])
        qk_c = sb("qk_c", [P, 16])
        tok = sb("tok", [P, NT, CW])
        junk_a, junk_l = sb("junk_a", [P, P]), sb("junk_l", [P, 2, HD])
        junk = sb("junk", [P, CW])
        region = cursor[0]
        gates, x_at = place("gates", [P, NT, 2 * D])
        x_in = sb("x_in", [P, NT, D], at=x_at)
        vecs = sb("vecs", [VROWS, D], at=x_at + 4 * NT * D)
        onehot = sb("onehot", [VROWS, RELS], at=x_at + 4 * NT * D + 4 * D)
        rel_aug = sb("rel_aug", [VROWS, H], at=x_at + 4 * NT * D + 4 * D + 4 * RELS)
        rel_row = sb("rel_row", [H, RELS], at=x_at + 4 * NT * D + 4 * D + 4 * RELS + 64)
        q_t = sb("q_t", [P, H, S])
        k_t = sb("k_t", [P, H, S])
        v_tok = sb("v_tok", [P, NT, D])
        glu_t = sb("glu_t", [P, KT, PAD + S])
        a_tok = sb("a_tok", [P, NT, D])
        bias = sb("bias", [P, H, S])
        probs = sb("probs", [P, 2, 2, S])
        probs_t = sb("probs_t", [P, 2, 2, P])
        gate_bias = sb("gate_bias", [P, 2, CW])
        glu = sb("glu", [P, NT, 256])
        sig = sb("sig", [P, NT, 256])
        st_max = sb("st_max", [P, NA, 2])
        st_sum = sb("st_sum", [P, NA, 2])
        st_rec = sb("st_rec", [P, NA, 2])
        st_mix = sb("st_mix", [P, NA])
        a_ss = sb("a_ss", [P, NA])
        a_ms = sb("a_ms", [P, NA])
        a_r = sb("a_r", [P, NA])
        ln_r = sb("ln_r", [P, S])
        assert cursor[0] <= nc.sbuf_usable_end, cursor[0]
        cursor[0] = region
        m_hi = sb("m_hi", [P, FK2, S], F32R)
        m_lo = sb("m_lo", [P, FK2, S], F32R)
        assert cursor[0] <= nc.sbuf_usable_end, cursor[0]
        ff_m = sb("ff_m", [P, NT, 256])
        ff_s = sb("ff_s", [P, NT, 256])
        mask = sb("mask", [P, ZC])
        neg_mask = sb("neg_mask", [P, ZC])
        neg_tri = sb("neg_tri", [P, P])
        neg_one = sb("neg_one", [P, P])
        coef = sb("coef", [P, CT2])
        sp_a = sb("sp_a", [P, 8, CT2])
        wr_g = sb("wr_g", [P, CT2, P])
        wi_g = sb("wi_g", [P, CT2, P])
        assert cursor[0] <= nc.sbuf_usable_end, cursor[0]
        cursor[0] = region
        q2_t = sb("q2_t", [P, CT2, S])
        k2_t = sb("k2_t", [P, CT2, S])
        v2 = sb("v2", [P, NT, W2])
        x2_tok, at = place("x2_tok", [P, NT, W2])
        r2 = sb("r2", [P, CT2, S], at=at)
        g2_tok = sb("g2_tok", [P, NT, W2])
        x2_t = sb("x2_t", [P, CT2, TAPS2 - 1 + S])
        u2 = sb("u2", [P, CT2, S])
        i2 = sb("i2", [P, CT2, S])
        a2 = sb("a2", [P, CT2, S])
        t2 = sb("t2", [P, CT2, S])
        g2_t = sb("g2_t", [P, CT2, S])
        soft = sb("soft", [P, 2, ZC])
        soft2 = sb("soft2", [P, 2, ZC])
        w2_t = sb("w2_t", [P, 8, ZC])
        assert cursor[0] <= region + 2 * 4 * FK2 * S, cursor[0]

        acc = ctx.enter_context(nc.psum_tensor("acc", [P, 2, NT, CW], F32))
        aux = ctx.enter_context(nc.psum_tensor("aux", [P, 4, CW], F32))
        rel_dram = nc.dram_tensor("rel_scratch", [H * P * RELS], F32, kind="Internal")

        raw_in = [sem(f"raw_in{i}") for i in range(RAW)]
        x_loaded = [sem(f"x_loaded{t}") for t in range(NT)]
        vecs_loaded, consts_loaded, lam_loaded = sem("vecs_loaded"), sem("consts_loaded"), sem("lam_loaded")
        rel_stored, bias_loaded = sem("rel_stored"), sem("bias_loaded")
        x_reloaded = sem("x_reloaded")
        gate_bias_in = [sem("gate_bias_in0"), sem("gate_bias_in1")]
        lru_w_in = sem("lru_w_in")
        stored = sem("stored")
        w_hi_ready, w_lo_dve, w_lo_pool, unit_done = sem("w_hi_ready"), sem("w_lo_dve"), sem("w_lo_pool"), sem("unit_done")
        ident_ready, zeros_ready, pool_consts = sem("ident_ready"), sem("zeros_ready"), sem("pool_consts")
        vec_turned, vec_ready = sem("vec_turned"), sem("vec_ready")
        rel_made, rel_kept, lam_sums, lam_exp, lam_ready = (sem("rel_made"), sem("rel_kept"), sem("lam_sums"),
                                                           sem("lam_exp"), sem("lam_ready"))
        stage_turned, stage_hi, stage_lo = sem("stage_turned"), sem("stage_hi"), sem("stage_lo")
        squares, mean_sq, rstd_ready, ms_parts = sem("squares"), sem("mean_sq"), sem("rstd_ready"), sem("ms_parts")
        sig_made, glu_made, glu_turned, glu_kept = sem("sig_made"), sem("glu_made"), sem("glu_turned"), sem("glu_kept")
        qk_sq, qk_sum, qk_pow, qk_coef, qk_normed = (sem("qk_sq"), sem("qk_sum"), sem("qk_pow"), sem("qk_coef"),
                                                     sem("qk_normed"))
        qk_turned, qk_kept, v_kept = sem("qk_turned"), sem("qk_kept"), sem("v_kept")
        conv_done = sem("conv_done")
        scored, biased, maxed, exped, summed, mixed = (sem("scored"), sem("biased"), sem("maxed"),
                                                               sem("exped"), sem("summed"), sem("mixed"))
        probs_turned, probs_kept, pv_done, a_kept, a_mean, a_pow, a_scaled = (
            sem("probs_turned"), sem("probs_kept"), sem("pv_done"), sem("a_kept"), sem("a_mean"), sem("a_pow"),
            sem("a_scaled"))
        a_turned, a_hi, a_lo = sem("a_turned"), sem("a_hi"), sem("a_lo")
        ln_sum, ln_centered, ln_sq, ln_var, ln_sd, ln_rec, ln_y, ln_act, c_hi_ready, c_lo_ready = (
            sem("ln_sum"), sem("ln_centered"), sem("ln_sq"), sem("ln_var"), sem("ln_sd"), sem("ln_rec"), sem("ln_y"),
            sem("ln_act"), sem("c_hi_ready"), sem("c_lo_ready"))
        gate_biased, gated, branch, branch_sum = sem("gate_biased"), sem("gated"), sem("branch"), sem("branch_sum")
        mix_turned, mix_hi, mix_lo = sem("mix_turned"), sem("mix_hi"), sem("mix_lo")
        added = sem("added")
        sp_made, a_squared, qk_reduced, lru_out = sem("sp_made"), sem("a_squared"), sem("qk_reduced"), sem("lru_out")
        ff_act, ff_made, ff_turned, ff_hi, ff_lo = (sem("ff_act"), sem("ff_made"), sem("ff_turned"), sem("ff_hi"),
                                                    sem("ff_lo"))
        up_act, up_sq, up_turned, up_hi, up_lo = sem("up_act"), sem("up_sq"), sem("up_turned"), sem("up_hi"), sem("up_lo")
        sp_act, sp_dve, coef_ready = sem("sp_act"), sem("sp_dve"), sem("coef_ready")
        x2_kept, x2_turned, x2_in, g2_kept, g2_turned, g2_in = (sem("x2_kept"), sem("x2_turned"), sem("x2_in"),
                                                               sem("g2_kept"), sem("g2_turned"), sem("g2_in"))
        pads_ready, u2_ready, ri_made, ri_kept = sem("pads_ready"), sem("u2_ready"), sem("ri_made"), sem("ri_kept")
        lru_act, lru_dve, lru_root, iu_ready, lru_hi, lru_lo = (sem("lru_act"), sem("lru_dve"), sem("lru_root"),
                                                                sem("iu_ready"), sem("lru_hi"), sem("lru_lo"))
        z_made, z_act, sp_ready, sfx_done, lw_ready, w2_ready, pv2_done, o2_hi, o2_lo = (
            sem("z_made"), sem("z_act"), sem("sp_ready"), sem("sfx_done"), sem("lw_ready"), sem("w2_ready"),
            sem("pv2_done"), sem("o2_hi"), sem("o2_lo"))
        gains_ready = sem("gains_ready")

        def f(ap):
            return ap.bitcast(F32)

        def vcol(row, kt):
            return vec_t[:, kt, row:row + 1]

        def again(ap, times):
            return bass.AP(tensor=ap.tensor, offset=ap.offset, ap=[ap.ap[0], [0, times], *ap.ap[1:]])

        def spread(ap, width):
            return bass.AP(tensor=ap.tensor, offset=ap.offset, ap=[*ap.ap, [0, width]])

        def acc_of(c, t):
            return acc[:, c % 2, t, :]

        def stage_of(kind, i):
            return i // 2 + 1

        def freed_by(c):
            kind, i = chunks[c][:2]
            order = [ch[1] for ch in chunks if ch[0] == kind].index(i)
            if kind in "qk":
                return qk_normed, 2 * QK.index((kind, i)) + 2
            return {"u": glu_made, "v": v_kept, "g": gate_biased, "pc": branch, "pa": branch, "res": added,
                    "ff": ff_made, "x2": x2_kept, "g2": g2_kept, "up": up_act}[kind], \
                2 * (order + 1) + (4 if kind == "pc" else 0)

        QK = [(ch[0], ch[1]) for ch in chunks if ch[0] in ("q", "k")]
        a_steps = {24: (0, 1), 27: (2, 3)}

        def pair_banks(n):
            return slice(2 * (n % 2), 2 * (n % 2) + 2)

        TURN2_BANK = [2, 3]
        LRU_BANK = [0, 1, 3, 0]

        block = ctx.enter_context(nc.Block())

        @block.sync
        def _(sp):
            x_rows = a["x"].rearrange("b (t p) d -> p (b t) d", p=P)
            for t in range(NT):
                sp.dma_start(x_in[:, t, :], x_rows[:, t, :]).then_inc(x_loaded[t], 16)
            for u, (c, k0, nk, _, _) in enumerate(units):
                _, _, w, col, pair, _, _ = chunks[c]
                n = w.shape[-1]
                if u >= RAW:
                    sp.wait_ge(w_hi_ready, u - RAW + 1)
                    sp.wait_ge(w_lo_pool if on_pool(u - RAW) else w_lo_dve, low_no[u - RAW])
                width = CW if pair is None else CW // 2
                for b in range(CW // width):
                    src = bass.AP(tensor=w.tensor, offset=w.offset + k0 * P * n + col + b * (pair or 0),
                                  ap=[[n, P], [P * n, nk], [1, width]])
                    sp.dma_start(raw[:, u % RAW, 0:nk, width * b:width * (b + 1)], src)\
                        .then_inc(raw_in[u % RAW], 16)
                if chunks[c][0] == "g" and k0 == 0:
                    i = chunks[c][1]
                    if i >= 2:
                        sp.wait_ge(gate_biased, 2 * (i - 1))
                    gb = a["gate_b"]
                    sp.dma_start(gate_bias[:, i % 2, :], bass.AP(tensor=gb.tensor, offset=gb.offset + CW * i,
                                                                 ap=[[0, P], [1, CW]])).then_inc(gate_bias_in[i % 2], 16)
                if u == begin["res", 0]:
                    sp.wait_ge(c_lo_ready, 2)
                    sp.wait_ge(c_hi_ready, 2)
                    sp.dma_start(x_res[:, :, :], x_rows).then_inc(x_reloaded, 16)
                if u == begin["res", 2]:
                    sp.wait_ge(pool_consts, 4)
                    for half in range(2):
                        for tile, w_g in ((wr_g, a["w_rg_2"]), (wi_g, a["w_ig_2"])):
                            ps = slice(HD * half, HD * half + HD)
                            src = w_g.rearrange("o (c b) i j -> b i (o c) j", b=2)[half]
                            sp.dma_start(tile[ps, :, ps], src).then_inc(lru_w_in, 16)
            o_rows = out.rearrange("b (t p) d -> p (b t) d", p=P)
            for i in range(2):
                for t in range(NT):
                    sp.wait_ge(added, 12 + 2 * i + t + 1)
                    sp.dma_start(o_rows[:, t, CW * i:CW * (i + 1)], x_res[:, t, CW * i:CW * (i + 1)]).then_inc(stored, 16)
            sp.wait_ge(stored, 16 * 2 * NT)

        @block.gpsimd
        def _(pool):
            nc.gpsimd.memset(ident[:, :], 0.0).then_inc(zeros_ready, 1)
            pool.wait_ge(zeros_ready, 1)
            nc.gpsimd.affine_select(out=ident[:, :], in_=ident[:, :], compare_op=ALU.not_equal, fill=1.0, base=0,
                                    pattern=[[-1, P]], channel_multiplier=1).then_inc(ident_ready, 1)
            nc.gpsimd.memset(nhalf[:, :], -0.5).then_inc(zeros_ready, 1)
            nc.gpsimd.memset(mean_w[:, :], 1.0 / D).then_inc(zeros_ready, 1)
            nc.gpsimd.memset(rel_aug[:, :], 0.0).then_inc(zeros_ready, 1)
            pool.wait_ge(zeros_ready, 4)
            nc.gpsimd.memset(rel_aug[BUCKETS:BUCKETS + 1, :], MASKED).then_inc(zeros_ready, 1)
            pool.dma_start(rel_aug[0:BUCKETS, :], a["rel_bias"]).then_inc(consts_loaded, 16)
            pool.dma_start(onehot[:, :], a["bucket_onehot"]).then_inc(consts_loaded, 16)
            for i, name in enumerate(("lam_q1", "lam_k1", "lam_q2", "lam_k2")):
                lv = a[name]
                pool.dma_start(lam_v[:, i, :], bass.AP(tensor=lv.tensor, offset=lv.offset, ap=[[0, P], [1, HD]]))\
                    .then_inc(lam_loaded, 16)
            pool.wait_ge(zeros_ready, 5)
            nc.gpsimd.memset(glu_t[:, :, 0:PAD], 0.0).then_inc(zeros_ready, 1)

            def power(out_, in_, s_in, n_in, s_out):
                pool.wait_ge(s_in, n_in)
                nc.gpsimd.tensor_tensor(out_, in_, nhalf[:, 0:in_.shape[1]], ALU.pow).then_inc(s_out, 1)

            power(rstd[:, 0, :], ms[:, 0, :], mean_sq, 1, rstd_ready)
            pool.wait_ge(rel_kept, 1)
            pool.dma_start(rel_dram.ap().rearrange("(h q r) -> h q r", h=H, q=P), again(rel_row[:, :], P))\
                .then_inc(rel_stored, 16)
            pool.wait_ge(rel_stored, 16)
            pool.dma_start(bias[:, :, :], bass.AP(tensor=rel_dram, offset=P - 1,
                                                  ap=[[RELS - 1, P], [RELS * P, H], [1, S]])).then_inc(bias_loaded, 16)

            for s in range(NU):
                if s in ended:
                    kind, i, c = ended[s]
                    if kind in ("q", "k"):
                        j = QK.index((kind, i))
                        power(qk_r[:, :], qk_ss[:, :], qk_sum, j + 1, qk_pow)
                    if kind == "res" and i % 2 == 1 and i < 7:
                        st = stage_of(kind, i)
                        power(rstd[:, st, :], ms[:, st, :], mean_sq, st + 1, rstd_ready)
                for g in range(2):
                    if s == ATT[8 * g + 7] + 4:
                        power(a_r[:, 8 * g:8 * g + 8], a_ms[:, 8 * g:8 * g + 8], a_mean, g + 1, a_pow)
                if s == begin["ff", 3]:
                    pool.wait_ge(stage_lo, 16)
                    nc.gpsimd.memset(mask[:, :], 1.0).then_inc(zeros_ready, 1)
                    nc.gpsimd.memset(neg_mask[:, :], 0.0).then_inc(zeros_ready, 1)
                    nc.gpsimd.memset(neg_tri[:, :], -1.0).then_inc(zeros_ready, 1)
                    nc.gpsimd.memset(neg_one[:, :], -1.0).then_inc(pool_consts, 1)
                    nc.gpsimd.memset(wr_g[:, :, :], 0.0).then_inc(pool_consts, 1)
                    nc.gpsimd.memset(wi_g[:, :, :], 0.0).then_inc(pool_consts, 1)
                    pool.wait_ge(zeros_ready, 9)
                    for k0 in (0, 2 * P):
                        nc.gpsimd.affine_select(out=mask[:, k0:k0 + P], in_=mask[:, k0:k0 + P], compare_op=ALU.is_gt,
                                                fill=0.0, base=0, pattern=[[1, P]], channel_multiplier=-1)\
                            .then_inc(zeros_ready, 1)
                        nc.gpsimd.affine_select(out=neg_mask[:, k0:k0 + P], in_=neg_mask[:, k0:k0 + P],
                                                compare_op=ALU.is_gt, fill=MASKED, base=0, pattern=[[1, P]],
                                                channel_multiplier=-1).then_inc(zeros_ready, 1)
                    nc.gpsimd.affine_select(out=neg_tri[:, :], in_=neg_tri[:, :], compare_op=ALU.is_ge, fill=0.0,
                                            base=0, pattern=[[-1, P]], channel_multiplier=1).then_inc(pool_consts, 1)
                if s == B:
                    pool.wait_ge(unit_done, B)
                    nc.gpsimd.memset(x2_t[:, :, 0:TAPS2 - 1], 0.0).then_inc(pads_ready, 1)
                u = s + LEAD
                if u < NU and on_pool(u):
                    nk = units[u][2]
                    pool.wait_ge(w_hi_ready, u + 1)
                    nc.gpsimd.tensor_tensor(w_lo[:, u % SPLIT, 0:nk, :], raw[:, u % RAW, 0:nk, :],
                                            f(w_hi[:, u % SPLIT, 0:nk, :]), ALU.subtract).then_inc(w_lo_pool, 1)

        @block.scalar
        def _(act):
            act.dma_start(vecs[:, :], a["vectors"]).then_inc(vecs_loaded, 16)

            def split_high(u):
                nk = units[u][2]
                act.wait_ge(raw_in[u % RAW], raw_value[u])
                if u >= SPLIT:
                    act.wait_ge(unit_done, u - SPLIT + 1)
                nc.scalar.activation(w_hi[:, u % SPLIT, 0:nk, :], raw[:, u % RAW, 0:nk, :], ACT.Copy)\
                    .then_inc(w_hi_ready, 1)

            def stage_high(st, g):
                act.wait_ge(stage_turned, 4 * st + g + 1)
                for j in range(2):
                    kt = 2 * g + j
                    nc.scalar.activation(h_hi[:, kt, :], aux[:, STAGE[g], 256 * j:256 * (j + 1)], ACT.Copy,
                                         scale=vcol(R_NORM[st], kt)).then_inc(stage_hi, 1)

            def pair_high(dst, g, bank, s_in, n_in, s_out, scale=1.0):
                act.wait_ge(s_in, n_in)
                nc.scalar.activation(dst[:, 2 * g:2 * g + 2, :], aux[:, bank, :].rearrange("p (a b) -> p a b", a=2),
                                     ACT.Copy, scale=scale).then_inc(s_out, 1)

            for t in range(NT):
                act.wait_ge(x_loaded[t], 16)
                for hf in range(2):
                    if t or hf:
                        act.wait_ge(squares, 2 * t + hf)
                    nc.scalar.activation(junk[:, :], x_in[:, t, CW * hf:CW * (hf + 1)], ACT.Square,
                                         accum_out=ss[:, 0, hf, t:t + 1]).then_inc(squares, 1)
            act.wait_ge(vec_turned, 1)
            nc.scalar.activation(vec_t[:, :, :], aux[:, 2, :].rearrange("p (a b) -> p a b", a=KT), ACT.Copy)\
                .then_inc(vec_ready, 1)
            act.wait_ge(vec_ready, 1)
            for g in range(4):
                stage_high(0, g)
            for u in range(LEAD):
                split_high(u)
            act.wait_ge(rel_made, 1)
            nc.scalar.activation(rel_row[:, :], aux[0:H, 2, 0:RELS], ACT.Copy).then_inc(rel_kept, 1)
            act.wait_ge(lam_sums, 2)
            nc.scalar.activation(small[:, 2:4], small[:, 0:2], ACT.Exp).then_inc(lam_exp, 1)
            nc.scalar.activation(gains[:, 0:1], vcol(R_SUB, 0), ACT.Copy, scale=1.0 - LAM_INIT).then_inc(gains_ready, 1)
            nc.scalar.activation(gains[:, 1:2], vcol(R_Q2, 0), ACT.Copy, scale=SC).then_inc(gains_ready, 1)

            def keep_qk(kind, i, t):
                j = QK.index((kind, i))
                act.wait_ge(qk_turned, 2 * j + t + 1)
                if i < 2:
                    dst = (q_t if kind == "q" else k_t)[:, 4 * i:4 * i + 4, P * t:P * (t + 1)]
                    gain = vcol(R_Q if kind == "q" else R_K, 0)
                else:
                    dst = (q2_t if kind == "q" else k2_t)[:, :, P * t:P * (t + 1)]
                    gain = gains[:, 1:2] if kind == "q" else vcol(R_K2, 0)
                    act.wait_ge(gains_ready, 2)
                nc.scalar.activation(dst, aux[:, 2, :].rearrange("p (a b) -> p a b", a=4), ACT.Copy, scale=gain)\
                    .then_inc(qk_kept, 1)

            def keep_glu(i, t):
                act.wait_ge(glu_turned, 2 * i + t + 1)
                nc.scalar.activation(glu_t[:, 2 * i:2 * i + 2, PAD + P * t:PAD + P * (t + 1)],
                                     aux[:, 2, 0:256].rearrange("p (a b) -> p a b", a=2), ACT.Copy).then_inc(glu_kept, 1)

            def softplus_parts(n):
                sf = (soft, soft2)[n % 2]
                act.wait_ge(z_made, n + 1)
                if n >= 2:
                    act.wait_ge(sp_made, n - 1)
                nc.scalar.activation(sf[:, :, :], aux[:, pair_banks(n), 0:ZC], ACT.Abs).then_inc(z_act, 1)
                if n == 0:
                    nc.scalar.add_instruction(mybir.InstLoadActFuncSet(name=nc.get_next_instruction_name(),
                                                                       act_func_set_id=EXP_LN_TABLES))
                act.wait_ge(z_act, 3 * n + 1)
                nc.scalar.activation(sf[:, :, :], sf[:, :, :], ACT.Exp, scale=-1.0).then_inc(z_act, 1)
                act.wait_ge(z_act, 3 * n + 2)
                nc.scalar.activation(sf[:, :, :], sf[:, :, :], ACT.Ln, bias=1.0).then_inc(z_act, 1)

            def weights2(n):
                act.wait_ge(lw_ready, n + 1)
                w2 = w2_t[:, 2 * n:2 * n + 2, :]
                nc.scalar.activation(w2, w2, ACT.Exp).then_inc(w2_ready, 1)

            def keep_turned2(dst, off, s_in, s_out):
                for t in range(NT):
                    act.wait_ge(s_in, t + 1)
                    nc.scalar.activation(dst[:, :, off + P * t:off + P * (t + 1)],
                                         aux[:, TURN2_BANK[t], :].rearrange("p (a b) -> p a b", a=4), ACT.Copy).then_inc(s_out, 1)

            for s in range(NU + 1):
                for i in range(FF // 256):
                    if s == end["ff", i] + 1:
                        pair_high(m_hi, i, i % 2, ff_turned, i + 1, ff_hi)
                for i in range(FF2 // CW):
                    if s == end["up", i] + 1:
                        for j in range(2):
                            pair_high(m_hi, 2 * i + j, j, up_turned, 2 * i + j + 1, up_hi)
                for at_, pairs in a_steps.items():
                    if s == at_ + 1:
                        for g in pairs:
                            if g == 0:
                                act.wait_ge(gains_ready, 1)
                            pair_high(c_hi, g, g % 2, a_turned, g + 1, a_hi, gains[:, 0:1])
                if s == end["pc", 0] + 1:
                    for g in range(2):
                        pair_high(c_hi, g, STAGE[g], mix_turned, g + 1, mix_hi)
                for i in (0, 2, 4):
                    if s == end["res", i] + 1:
                        stage_high(i // 2 + 1, 0)
                        stage_high(i // 2 + 1, 1)
                for n in range(NA):
                    if s == ATT[n] + 3:
                        act.wait_ge(probs_turned, n + 1)
                        if n >= 2:
                            act.wait_ge(pv_done, n - 1)
                        nk = n % 2 + 1
                        nc.scalar.activation(probs_t[:, n % 2, 0:nk, :],
                                             aux[:, 3, 0:P * nk].rearrange("p (a b) -> p a b", a=nk), ACT.Copy)\
                            .then_inc(probs_kept, 1)
                if (s < LN or s >= B) and s + LEAD < NU:
                    split_high(s + LEAD)
                for n in range(NA):
                    if s == ATT[n] + 1:
                        K = P * (n % 2 + 1)
                        act.wait_ge(maxed, n + 1)
                        for m in range(2):
                            pr = probs[:, n % 2, m, 0:K]
                            nc.scalar.activation(pr, pr, ACT.Exp, bias=st_max[:, n, m:m + 1],
                                                 accum_out=st_sum[:, n, m:m + 1]).then_inc(exped, 1)
                if s in ended:
                    kind, i, c = ended[s]
                    act.wait_ge(unit_done, last[c] + 1)
                    blk = 0 if c <= number["g", 3] else 2 if c >= number["x2", 0] else 1
                    if kind in ("u", "q", "k", "v", "x2", "g2"):
                        act.wait_ge(rstd_ready, blk + 1)
                    for t in range(NT):
                        r = rstd[:, blk, t:t + 1]
                        if kind == "u":
                            if i:
                                act.wait_ge(glu_made, 2 * (i - 1) + t + 1)
                            nc.scalar.activation(sig[:, t, :], acc_of(c, t)[:, 256:512], ACT.Sigmoid, scale=r)\
                                .then_inc(sig_made, 1)
                        if kind in ("q", "k"):
                            j = QK.index((kind, i))
                            if j:
                                act.wait_ge(qk_turned, 2 * (j - 1) + t + 1)
                            nc.scalar.activation(tok[:, t, :], acc_of(c, t), ACT.Square, scale=r).then_inc(qk_sq, 1)
                        if kind == "v":
                            dst = v_tok[:, t, CW * i:CW * (i + 1)] if i < 2 else v2[:, t, :]
                            nc.scalar.activation(dst, acc_of(c, t), ACT.Copy, scale=r).then_inc(v_kept, 1)
                        if kind == "x2":
                            nc.scalar.activation(x2_tok[:, t, :], acc_of(c, t), ACT.Copy, scale=r).then_inc(x2_kept, 1)
                        if kind == "g2":
                            nc.scalar.activation(g2_tok[:, t, :], acc_of(c, t), ACT.Gelu_apprx_tanh, scale=r)\
                                .then_inc(g2_kept, 1)
                        if kind == "g":
                            act.wait_ge(gate_biased, 2 * i + t + 1)
                            gt = gates[:, t, CW * i:CW * (i + 1)]
                            nc.scalar.activation(gt, gt, ACT.Sigmoid).then_inc(gated, 1)
                        if kind == "ff":
                            act.wait_ge(rstd_ready, 2)
                            if i:
                                act.wait_ge(ff_made, 2 * (i - 1) + t + 1)
                            nc.scalar.activation(ff_s[:, t, :], acc_of(c, t)[:, 0:256], ACT.Silu,
                                                 scale=rstd[:, 1, t:t + 1]).then_inc(ff_act, 1)
                        if kind == "up":
                            act.wait_ge(rstd_ready, 4)
                            if i:
                                act.wait_ge(up_turned, 2 * i)
                            nc.scalar.activation(tok[:, t, :], acc_of(c, t), ACT.Relu, scale=rstd[:, 3, t:t + 1])\
                                .then_inc(up_act, 1)
                        if kind == "res" and i < 6:
                            n = 4 + 2 * i + t
                            act.wait_ge(squares, n)
                            act.wait_ge(added, 2 * i + t + 1)
                            nc.scalar.activation(junk[:, :], x_res[:, t, CW * (i % 2):CW * (i % 2 + 1)], ACT.Square,
                                                 accum_out=ss[:, i // 2 + 1, i % 2, t:t + 1]).then_inc(squares, 1)
                if LN <= s < B and s + LEAD < NU:
                    split_high(s + LEAD)
                for i in range(4):
                    if s == end["u", i] + 1:
                        keep_glu(i, 0)
                        keep_glu(i, 1)
                for kind, i in QK:
                    if s == end[kind, i] + 2:
                        keep_qk(kind, i, 1)
                for kind, i in QK:
                    if s == end[kind, i] + 1:
                        keep_qk(kind, i, 0)
                for n in range(NA):
                    if s == ATT[n] + 3:
                        act.wait_ge(pv_done, n + 1)
                        hd, qb = n // 2, n % 2
                        if n:
                            act.wait_ge(a_squared, n)
                        nc.scalar.activation(junk_a[:, :], aux[:, 3, 0:P], ACT.Square,
                                             scale=st_rec[:, n, 0:1], accum_out=a_ss[:, n:n + 1]).then_inc(a_squared, 1)
                        nc.scalar.activation(a_tok[:, qb, P * hd:P * (hd + 1)], aux[:, 3, 0:P], ACT.Copy,
                                             scale=st_rec[:, n, 0:1]).then_inc(a_kept, 1)
                if s == end["pc", 1]:
                    for g in (2, 3):
                        pair_high(c_hi, g, STAGE[g], mix_turned, g + 1, mix_hi)
                for i in (1, 3, 5):
                    if s == end["res", i]:
                        stage_high(i // 2 + 1, 2)
                        stage_high(i // 2 + 1, 3)
                if s == LN + 1:
                    for hf in range(2):
                        act.wait_ge(ln_centered, hf + 1)
                        nc.scalar.activation(c_sq[:, 4 * hf:4 * hf + 4, :], conv[:, 4 * hf:4 * hf + 4, :], ACT.Square)\
                            .then_inc(ln_sq, 1)
                if s == LN + 2:
                    act.wait_ge(ln_var, 1)
                    nc.scalar.activation(ln_r[:, :], ln_r[:, :], ACT.Sqrt).then_inc(ln_sd, 1)
                    for hf in range(2):
                        act.wait_ge(ln_y, hf + 1)
                        for kt in range(4 * hf, 4 * hf + 4):
                            nc.scalar.activation(conv[:, kt, :], conv[:, kt, :], ACT.Silu, bias=vcol(R_LN_B, kt),
                                                 scale=vcol(R_LN_W, kt)).then_inc(ln_act, 1)
                        act.wait_ge(ln_act, 4 * hf + 4)
                        nc.scalar.activation(h_hi[:, 4 * hf:4 * hf + 4, :], conv[:, 4 * hf:4 * hf + 4, :], ACT.Copy)\
                            .then_inc(c_hi_ready, 1)
                if s == begin["res", 2]:
                    nc.scalar.activation(sp_a[:, 0, :], vec_t[:, 0:CT2, R_LAMBDA], ACT.Abs).then_inc(sp_act, 1)
                    act.wait_ge(sp_act, 1)
                    nc.scalar.activation(sp_a[:, 1, :], sp_a[:, 0, :], ACT.Exp, scale=-1.0).then_inc(sp_act, 1)
                if s == B + 3:
                    keep_turned2(x2_t, TAPS2 - 1, x2_turned, x2_in)
                for ct in range(CT2):
                    if s == (B + 5 if ct < 3 else B + 6):
                        act.wait_ge(ri_made, ct + 1)
                        bank = LRU_BANK[ct]
                        nc.scalar.activation(r2[:, ct, :], aux[:, bank, 0:256], ACT.Sigmoid, bias=vcol(R_RG, ct))\
                            .then_inc(ri_kept, 1)
                        nc.scalar.activation(i2[:, ct, :], aux[:, bank, 256:512], ACT.Sigmoid, bias=vcol(R_IG, ct))\
                            .then_inc(ri_kept, 1)
                if s == B + 6:
                    act.wait_ge(coef_ready, 1)
                    act.wait_ge(ri_kept, 2 * CT2)
                    for ct in range(CT2):
                        nc.scalar.activation(t2[:, ct, :], r2[:, ct, :], ACT.Tanh, scale=coef[:, ct:ct + 1])\
                            .then_inc(lru_act, 1)
                    for ct in range(CT2):
                        nc.scalar.activation(a2[:, ct, :], r2[:, ct, :], ACT.Exp, scale=coef[:, ct:ct + 1])\
                            .then_inc(lru_act, 1)
                if s == B + 7:
                    act.wait_ge(lru_dve, 2)
                    nc.scalar.activation(t2[:, :, :], t2[:, :, :], ACT.Sqrt, scale=-1.0).then_inc(lru_root, 1)
                if s == B + 8:
                    softplus_parts(0)
                if s == B + 9:
                    keep_turned2(g2_t, 0, g2_turned, g2_in)
                    softplus_parts(1)
                    act.wait_ge(lru_out, 1)
                    nc.scalar.activation(c_hi[:, CT2:KT, :], t2[:, :, :], ACT.Copy).then_inc(lru_hi, 1)
                    weights2(0)
                if s == B + 10:
                    softplus_parts(2)
                    weights2(1)
                    softplus_parts(3)
                if s == B + 11:
                    weights2(2)
                    weights2(3)
                    for n in range(4):
                        act.wait_ge(pv2_done, n + 1)
                        nc.scalar.activation(c_hi[:, n, :], aux[:, n, 0:S], ACT.Copy).then_inc(o2_hi, 1)

        @block.vector
        def _(dve):
            def split_low(u):
                nk = units[u][2]
                dve.wait_ge(w_hi_ready, u + 1)
                nc.vector.tensor_tensor(w_lo[:, u % SPLIT, 0:nk, :], raw[:, u % RAW, 0:nk, :],
                                        f(w_hi[:, u % SPLIT, 0:nk, :]), ALU.subtract).then_inc(w_lo_dve, 1)

            def stage_low(st, g):
                for j in range(2):
                    kt = 2 * g + j
                    if j == 0:
                        dve.wait_ge(stage_hi, 8 * st + 2 * g + 2)
                    nc.vector.scalar_tensor_tensor(out=h_lo[:, kt, :], in0=aux[:, STAGE[g], 256 * j:256 * (j + 1)],
                                                   scalar=vcol(R_NORM[st], kt), in1=f(h_hi[:, kt, :]), op0=ALU.mult,
                                                   op1=ALU.subtract).then_inc(stage_lo, 1)

            def pair_low(hi, lo, g, bank, s_in, n_in, s_out):
                dve.wait_ge(s_in, n_in)
                nc.vector.tensor_tensor(lo[:, 2 * g:2 * g + 2, :], aux[:, bank, :].rearrange("p (a b) -> p a b", a=2),
                                        f(hi[:, 2 * g:2 * g + 2, :]), ALU.subtract).then_inc(s_out, 1)

            def mean_square(st):
                dve.wait_ge(squares, 4 * st + 4)
                nc.vector.tensor_tensor(ms[:, st, :], ss[:, st, 0, :], ss[:, st, 1, :], ALU.add).then_inc(ms_parts, 1)
                dve.wait_ge(ms_parts, st + 1)
                nc.vector.tensor_scalar(ms[:, st, :], ms[:, st, :], 1.0 / D, EPS, ALU.mult, ALU.add).then_inc(mean_sq, 1)

            def conv_step(o):
                pair, tap, ct = o // (2 * TAPS), o % (2 * TAPS) // 2, 2 * (o // (2 * TAPS)) + o % 2
                if o % (2 * TAPS) == 0:
                    dve.wait_ge(glu_kept, 2 * pair + 2)
                    if o == 0:
                        dve.wait_ge(zeros_ready, 6)
                if tap == 0:
                    nc.vector.tensor_scalar(conv[:, ct, :], glu_t[:, ct, 0:S], vcol(R_CONV_W, ct), vcol(R_CONV_B, ct),
                                            ALU.mult, ALU.add).then_inc(conv_done, 1)
                else:
                    dve.wait_ge(conv_done, o - 1)
                    nc.vector.scalar_tensor_tensor(out=conv[:, ct, :], in0=glu_t[:, ct, tap:tap + S],
                                                   scalar=vcol(R_CONV_W + tap, ct), in1=conv[:, ct, :], op0=ALU.mult,
                                                   op1=ALU.add).then_inc(conv_done, 1)

            def softplus_sum(n):
                dve.wait_ge(z_act, 3 * n + 3)
                if n == 0:
                    dve.wait_ge(pool_consts, 4)
                w2 = w2_t[:, 2 * n:2 * n + 2, :]
                nc.vector.scalar_tensor_tensor(out=w2, in0=aux[:, pair_banks(n), 0:ZC], scalar=0.0,
                                               in1=(soft, soft2)[n % 2][:, :, :], op0=ALU.max, op1=ALU.add)\
                    .then_inc(sp_made, 1)
                dve.wait_ge(sp_made, n + 1)
                nc.vector.tensor_tensor(w2, w2, again(mask[:, :], 2), ALU.mult).then_inc(sp_ready, 1)

            def log_weights(n):
                dve.wait_ge(sfx_done, n + 1)
                nc.vector.scalar_tensor_tensor(out=w2_t[:, 2 * n:2 * n + 2, :], in0=aux[:, pair_banks(n), 0:ZC],
                                               scalar=0.0, in1=again(neg_mask[:, :], 2), op0=ALU.min, op1=ALU.add)\
                    .then_inc(lw_ready, 1)

            def pv2_low(n):
                dve.wait_ge(o2_hi, n + 1)
                nc.vector.tensor_tensor(c_lo[:, n, :], aux[:, n, 0:S], f(c_hi[:, n, :]), ALU.subtract)\
                    .then_inc(o2_lo, 1)

            mean_square(0)
            dve.wait_ge(vec_ready, 1)
            for g in range(4):
                stage_low(0, g)
            for u in range(LEAD):
                split_low(u)
            dve.wait_ge(lam_loaded, 64)
            for i in range(2):
                nc.vector.tensor_tensor_reduce(junk_l[:, i, :], lam_v[:, 2 * i, :], lam_v[:, 2 * i + 1, :], 1.0, 0.0,
                                               ALU.mult, ALU.add, small[:, i:i + 1]).then_inc(lam_sums, 1)
            dve.wait_ge(lam_exp, 1)
            nc.vector.scalar_tensor_tensor(out=small[:, 4:5], in0=small[:, 3:4], scalar=LAM_INIT, in1=small[:, 2:3],
                                           op0=ALU.subtract, op1=ALU.subtract).then_inc(lam_ready, 1)
            taps_done = 0
            for s in range(NU + 1):
                for i in range(FF // 256):
                    if s == end["ff", i] + 1:
                        pair_low(m_hi, m_lo, i, i % 2, ff_hi, i + 1, ff_lo)
                for i in range(FF2 // CW):
                    if s == end["up", i] + 1:
                        for j in range(2):
                            pair_low(m_hi, m_lo, 2 * i + j, j, up_hi, 2 * i + j + 1, up_lo)
                for at_, pairs in a_steps.items():
                    if s == at_ + 1:
                        for g in pairs:
                            dve.wait_ge(a_hi, g + 1)
                            nc.vector.scalar_tensor_tensor(
                                out=c_lo[:, 2 * g:2 * g + 2, :], in0=aux[:, g % 2, :].rearrange("p (a b) -> p a b", a=2),
                                scalar=gains[:, 0:1], in1=f(c_hi[:, 2 * g:2 * g + 2, :]), op0=ALU.mult,
                                op1=ALU.subtract).then_inc(a_lo, 1)
                if s == end["pc", 0] + 1:
                    for g in range(2):
                        pair_low(c_hi, c_lo, g, STAGE[g], mix_hi, g + 1, mix_lo)
                for i in (0, 2, 4):
                    if s == end["res", i] + 1:
                        stage_low(i // 2 + 1, 0)
                        stage_low(i // 2 + 1, 1)
                for n in range(NA):
                    if s == ATT[n] + 1:
                        hd, qb = n // 2, n % 2
                        K = P * (qb + 1)
                        dve.wait_ge(scored, n + 1)
                        if n == 0:
                            dve.wait_ge(bias_loaded, 16)
                        if n >= 2:
                            dve.wait_ge(probs_turned, n - 1)
                        pr = probs[:, n % 2, :, 0:K]
                        nc.vector.scalar_tensor_tensor(
                            out=pr, in0=aux[:, 0:2, 0:K], scalar=SC,
                            in1=again(bias[:, hd, S - K:S], 2), op0=ALU.mult, op1=ALU.add).then_inc(biased, 1)
                        dve.wait_ge(biased, n + 1)
                        nc.vector.tensor_reduce(st_max[:, n, :], pr, AX.X, ALU.max, negate=True).then_inc(maxed, 1)
                for _ in range(min(quota[s], 4)):
                    conv_step(taps_done)
                    taps_done += 1
                if s in ended:
                    kind, i, c = ended[s]
                    dve.wait_ge(unit_done, last[c] + 1)
                    blk = 0 if c <= number["g", 3] else 2 if c >= number["x2", 0] else 1
                    for t in range(NT):
                        r = rstd[:, blk, t:t + 1]
                        if kind == "u":
                            dve.wait_ge(sig_made, 2 * i + t + 1)
                            if i:
                                dve.wait_ge(glu_turned, 2 * (i - 1) + t + 1)
                            nc.vector.scalar_tensor_tensor(out=glu[:, t, :], in0=acc_of(c, t)[:, 0:256], scalar=r,
                                                           in1=sig[:, t, :], op0=ALU.mult, op1=ALU.mult)\
                                .then_inc(glu_made, 1)
                        if kind in ("q", "k"):
                            j = QK.index((kind, i))
                            dve.wait_ge(qk_sq, 2 * j + t + 1)
                            nc.vector.tensor_reduce(qk_ss[:, 8 * t:8 * t + 8],
                                                    tok[:, t, :].rearrange("p (a b) -> p a b", b=HD), AX.X, ALU.add)\
                                .then_inc(qk_reduced, 1)
                        if kind == "g":
                            dve.wait_ge(rstd_ready, 1)
                            dve.wait_ge(gate_bias_in[i % 2], 16 * (i // 2 + 1))
                            nc.vector.scalar_tensor_tensor(out=gates[:, t, CW * i:CW * (i + 1)], in0=acc_of(c, t),
                                                           scalar=r, in1=gate_bias[:, i % 2, :], op0=ALU.mult,
                                                           op1=ALU.add).then_inc(gate_biased, 1)
                        if kind == "pc":
                            dve.wait_ge(gated, 2 * (2 + i) + t + 1)
                            gt = gates[:, t, D + CW * i:D + CW * (i + 1)]
                            nc.vector.tensor_tensor(gt, acc_of(c, t), gt, ALU.mult).then_inc(branch, 1)
                        if kind == "pa":
                            dve.wait_ge(gated, 2 * i + t + 1)
                            gt = gates[:, t, CW * i:CW * (i + 1)]
                            nc.vector.tensor_tensor(gt, acc_of(c, t), gt, ALU.mult).then_inc(branch, 1)
                        if kind == "ff":
                            dve.wait_ge(ff_act, 2 * i + t + 1)
                            if i:
                                dve.wait_ge(ff_turned, i)
                            nc.vector.scalar_tensor_tensor(out=ff_m[:, t, :], in0=acc_of(c, t)[:, 256:512],
                                                           scalar=rstd[:, 1, t:t + 1], in1=ff_s[:, t, :], op0=ALU.mult,
                                                           op1=ALU.mult).then_inc(ff_made, 1)
                        if kind == "up":
                            dve.wait_ge(up_act, 2 * i + t + 1)
                            nc.vector.tensor_tensor(tok[:, t, :], tok[:, t, :], tok[:, t, :], ALU.mult)\
                                .then_inc(up_sq, 1)
                        if kind == "res":
                            if i == 0:
                                dve.wait_ge(x_reloaded, 16)
                            xr = x_res[:, t, CW * (i % 2):CW * (i % 2 + 1)]
                            nc.vector.tensor_tensor(xr, acc_of(c, t), xr, ALU.add).then_inc(added, 1)
                    if kind in ("q", "k"):
                        j = QK.index((kind, i))
                        dve.wait_ge(qk_reduced, 2 * j + 2)
                        nc.vector.tensor_scalar(qk_ss[:, :], qk_ss[:, :], 1.0 / HD, EPS, ALU.mult, ALU.add)\
                            .then_inc(qk_sum, 1)
                    if kind == "pc":
                        for t in range(NT):
                            dve.wait_ge(branch, 4 + 2 * i + t + 1)
                            gt = gates[:, t, CW * i:CW * (i + 1)]
                            nc.vector.tensor_tensor(gt, gt, gates[:, t, D + CW * i:D + CW * (i + 1)], ALU.add)\
                                .then_inc(branch_sum, 1)
                if s + LEAD < NU and not on_pool(s + LEAD):
                    split_low(s + LEAD)
                for n in range(NA):
                    if s == ATT[n] + 1:
                        K = P * (n % 2 + 1)
                        dve.wait_ge(exped, 2 * n + 2)
                        nc.vector.reciprocal(st_rec[:, n, :], st_sum[:, n, :]).then_inc(summed, 1)
                        dve.wait_ge(summed, 2 * n + 1)
                        if n == 0:
                            dve.wait_ge(lam_ready, 1)
                        nc.vector.scalar_tensor_tensor(out=st_mix[:, n:n + 1], in0=st_sum[:, n, 0:1],
                                                       scalar=small[:, 4:5], in1=st_rec[:, n, 1:2], op0=ALU.mult,
                                                       op1=ALU.mult).then_inc(summed, 1)
                for _ in range(max(0, min(quota[s] - 4, 3))):
                    conv_step(taps_done)
                    taps_done += 1
                for n in range(NA):
                    if s == ATT[n] + 1:
                        K = P * (n % 2 + 1)
                        dve.wait_ge(summed, 2 * n + 2)
                        nc.vector.scalar_tensor_tensor(out=probs[:, n % 2, 0, 0:K], in0=probs[:, n % 2, 1, 0:K],
                                                       scalar=st_mix[:, n:n + 1], in1=probs[:, n % 2, 0, 0:K],
                                                       op0=ALU.mult, op1=ALU.add).then_inc(mixed, 1)
                for _ in range(max(0, quota[s] - 7)):
                    conv_step(taps_done)
                    taps_done += 1
                if s in ended and ended[s][0] in ("q", "k"):
                    kind, i, c = ended[s]
                    j = QK.index((kind, i))
                    dve.wait_ge(qk_pow, j + 1)
                    for t in range(NT):
                        nc.vector.tensor_scalar(qk_c[:, 8 * t:8 * t + 8], qk_r[:, 8 * t:8 * t + 8],
                                                rstd[:, blk, t:t + 1], None, ALU.mult).then_inc(qk_coef, 1)
                    for t in range(NT):
                        dve.wait_ge(qk_coef, 2 * j + t + 1)
                        nc.vector.tensor_tensor(tok[:, t, :].rearrange("p (a b) -> p a b", b=HD),
                                                acc_of(c, t).rearrange("p (a b) -> p a b", b=HD),
                                                spread(qk_c[:, 8 * t:8 * t + 8], HD), ALU.mult).then_inc(qk_normed, 1)
                for g in range(2):
                    if s == ATT[8 * g + 7] + 4:
                        dve.wait_ge(a_squared, 8 * g + 8)
                        dve.wait_ge(a_kept, 8 * g + 8)
                        nc.vector.tensor_scalar(a_ms[:, 8 * g:8 * g + 8], a_ss[:, 8 * g:8 * g + 8], 1.0 / P, EPS,
                                                ALU.mult, ALU.add).then_inc(a_mean, 1)
                        dve.wait_ge(a_pow, g + 1)
                        for qb in range(2):
                            at_ = a_tok[:, qb, CW * g:CW * (g + 1)].rearrange("p (a b) -> p a b", b=P)
                            rr = a_r[:, 8 * g:8 * g + 8].rearrange("p (a b) -> p b a", b=2)[:, qb, :]
                            nc.vector.tensor_tensor(at_, at_, spread(rr, P), ALU.mult).then_inc(a_scaled, 1)
                if s == end["pc", 1]:
                    for g in (2, 3):
                        pair_low(c_hi, c_lo, g, STAGE[g], mix_hi, g + 1, mix_lo)
                for i in (1, 3, 5):
                    if s == end["res", i]:
                        stage_low(i // 2 + 1, 2)
                        stage_low(i // 2 + 1, 3)
                        mean_square(i // 2 + 1)
                if s == LN + 1:
                    dve.wait_ge(ln_sum, 1)
                    for hf in range(2):
                        ch = conv[:, 4 * hf:4 * hf + 4, :]
                        nc.vector.tensor_tensor(ch, ch, again(aux[:, 2, 0:S], 4), ALU.subtract).then_inc(ln_centered, 1)
                if s == LN + 2:
                    dve.wait_ge(ln_sum, 2)
                    nc.vector.tensor_scalar(ln_r[:, :], aux[:, 2, 0:S], EPS, None, ALU.add).then_inc(ln_var, 1)
                    dve.wait_ge(ln_sd, 1)
                    nc.vector.reciprocal(ln_r[:, :], ln_r[:, :]).then_inc(ln_rec, 1)
                    dve.wait_ge(ln_rec, 1)
                    for hf in range(2):
                        ch = conv[:, 4 * hf:4 * hf + 4, :]
                        nc.vector.tensor_tensor(ch, ch, again(ln_r[:, :], 4), ALU.mult).then_inc(ln_y, 1)
                    for hf in range(2):
                        dve.wait_ge(c_hi_ready, hf + 1)
                        nc.vector.tensor_tensor(h_lo[:, 4 * hf:4 * hf + 4, :], conv[:, 4 * hf:4 * hf + 4, :],
                                                f(h_hi[:, 4 * hf:4 * hf + 4, :]), ALU.subtract).then_inc(c_lo_ready, 1)
                if s == begin["res", 2]:
                    steps = [0]

                    def link(ins):
                        steps[0] += 1
                        ins.then_inc(sp_dve, 1)
                        dve.wait_ge(sp_dve, steps[0])

                    lam_c, e, den, z, z2, p_ = (vec_t[:, 0:CT2, R_LAMBDA], *(sp_a[:, k, :] for k in (1, 2, 3, 4, 5)))
                    dve.wait_ge(sp_act, 2)
                    link(nc.vector.tensor_scalar(den, e, 2.0, None, ALU.add))
                    link(nc.vector.reciprocal(den, den))
                    link(nc.vector.tensor_tensor(z, e, den, ALU.mult))
                    link(nc.vector.tensor_tensor(z2, z, z, ALU.mult))
                    link(nc.vector.tensor_scalar(p_, z2, 1.0 / 15, None, ALU.mult))
                    for k in (13, 11, 9, 7, 5, 3):
                        link(nc.vector.scalar_tensor_tensor(out=p_, in0=p_, scalar=1.0 / k, in1=z2, op0=ALU.add,
                                                            op1=ALU.mult))
                    link(nc.vector.scalar_tensor_tensor(out=p_, in0=p_, scalar=1.0, in1=z, op0=ALU.add, op1=ALU.mult))
                    link(nc.vector.tensor_scalar(den, lam_c, -1.0, 0.0, ALU.mult, ALU.max))
                    link(nc.vector.scalar_tensor_tensor(out=p_, in0=p_, scalar=2.0, in1=den, op0=ALU.mult, op1=ALU.add))
                    nc.vector.tensor_scalar(coef[:, :], p_, -LRU_C, None, ALU.mult).then_inc(coef_ready, 1)
                if s in (B + 3, B + 4):
                    dve.wait_ge(x2_in, 2)
                    dve.wait_ge(pads_ready, 1)
                    for tap in range(2 * (s - B - 3), 2 * (s - B - 3) + 2):
                        for ct in range(CT2):
                            if tap == 0:
                                nc.vector.tensor_scalar(u2[:, ct, :], x2_t[:, ct, 0:S], vcol(R_CONV2_W, ct),
                                                        vcol(R_CONV2_B, ct), ALU.mult, ALU.add).then_inc(u2_ready, 1)
                            else:
                                dve.wait_ge(u2_ready, CT2 * (tap - 1) + ct + 1)
                                nc.vector.scalar_tensor_tensor(out=u2[:, ct, :], in0=x2_t[:, ct, tap:tap + S],
                                                               scalar=vcol(R_CONV2_W + tap, ct), in1=u2[:, ct, :],
                                                               op0=ALU.mult, op1=ALU.add).then_inc(u2_ready, 1)
                if s == B + 6:
                    dve.wait_ge(ri_kept, 2 * CT2)
                    nc.vector.tensor_tensor(i2[:, :, :], i2[:, :, :], u2[:, :, :], ALU.mult).then_inc(iu_ready, 1)
                    dve.wait_ge(lru_act, 2 * CT2)
                    nc.vector.tensor_tensor(r2[:, :, :], a2[:, :, :], a2[:, :, :], ALU.mult).then_inc(lru_dve, 1)
                    dve.wait_ge(lru_dve, 1)
                    nc.vector.scalar_tensor_tensor(out=t2[:, :, :], in0=r2[:, :, :], scalar=1.0, in1=t2[:, :, :],
                                                   op0=ALU.add, op1=ALU.mult).then_inc(lru_dve, 1)
                if s == B + 8:
                    dve.wait_ge(lru_root, 1)
                    dve.wait_ge(iu_ready, 1)
                    nc.vector.tensor_tensor(i2[:, :, :], i2[:, :, :], t2[:, :, :], ALU.mult).then_inc(lru_dve, 1)
                    dve.wait_ge(lru_dve, 3)
                    for ct in range(CT2):
                        nc.vector.tensor_tensor_scan(u2[:, ct, :], a2[:, ct, :], i2[:, ct, :], 0.0, ALU.mult, ALU.add)\
                            .then_inc(lru_dve, 1)
                    softplus_sum(0)
                if s == B + 9:
                    dve.wait_ge(lru_dve, 3 + CT2)
                    dve.wait_ge(g2_in, 2)
                    nc.vector.tensor_tensor(t2[:, :, :], u2[:, :, :], g2_t[:, :, :], ALU.mult).then_inc(lru_out, 1)
                    log_weights(0)
                    softplus_sum(1)
                    dve.wait_ge(lru_hi, 1)
                    nc.vector.tensor_tensor(c_lo[:, CT2:KT, :], t2[:, :, :], f(c_hi[:, CT2:KT, :]), ALU.subtract)\
                        .then_inc(lru_lo, 1)
                if s == B + 10:
                    log_weights(1)
                    softplus_sum(2)
                    softplus_sum(3)
                    log_weights(2)
                if s == B + 11:
                    log_weights(3)
                    for n in range(4):
                        pv2_low(n)

        @block.tensor
        def _(pe):
            held = {}

            def claim(places, sem_, value):
                for p_ in places:
                    if p_ in held:
                        pe.wait_ge(*held[p_])
                    held[p_] = (sem_, value)

            def turn(out_, in_):
                return nc.tensor.transpose(out_, in_, ident[:, :])

            def turn_pair(src, g, bank):
                for j in range(2):
                    for t in range(NT):
                        kt = 2 * g + j
                        mm = turn(aux[:, bank, 256 * j + P * t:256 * j + P * (t + 1)], src[:, t, P * kt:P * (kt + 1)])
                return mm

            def turn_four(src, bank=2):
                for k in range(4):
                    mm = turn(aux[:, bank, P * k:P * (k + 1)], src[:, P * k:P * (k + 1)])
                return mm

            def stage(st, pairs):
                src = x_res if st else x_in
                for g in pairs:
                    claim([STAGE[g]], stage_lo, 8 * st + 2 * g + 2)
                    turn_pair(src, g, STAGE[g]).then_inc(stage_turned, 1)

            def turn_glu(i, t):
                pe.wait_ge(glu_made, 2 * i + t + 1)
                claim([2], glu_kept, 2 * i + t + 1)
                for j in range(2):
                    mm = turn(aux[:, 2, P * j:P * (j + 1)], glu[:, t, P * j:P * (j + 1)])
                mm.then_inc(glu_turned, 1)

            def turn_qk(kind, i, t):
                j = QK.index((kind, i))
                pe.wait_ge(qk_normed, 2 * j + t + 1)
                claim([2], qk_kept, 2 * j + t + 1)
                turn_four(tok[:, t, :]).then_inc(qk_turned, 1)

            def scores(n):
                hd, qb = n // 2, n % 2
                if n in (0, 8):
                    pe.wait_ge(qk_kept, 4 * (n // 8) + 4)
                claim([0, 1], biased, n + 1)
                for m in range(2):
                    ps = slice(HD * m, HD * (m + 1))
                    mm = nc.tensor.matmul(aux[:, m, 0:P * (qb + 1)], q_t[ps, hd, P * qb:P * (qb + 1)],
                                          k_t[ps, hd, 0:P * (qb + 1)], start=True, stop=True)
                mm.then_inc(scored, 1)

            def turn_probs(n):
                pe.wait_ge(mixed, n + 1)
                claim([3], probs_kept, n + 1)
                for k in range(n % 2 + 1):
                    mm = turn(aux[:, 3, P * k:P * (k + 1)], probs[:, n % 2, 0, P * k:P * (k + 1)])
                mm.then_inc(probs_turned, 1)

            def attend(n):
                hd, qb = n // 2, n % 2
                pe.wait_ge(probs_kept, n + 1)
                pe.wait_ge(v_kept, 2 * (hd // 4) + 2)
                claim([3], a_kept, n + 1)
                for k in range(qb + 1):
                    mm = nc.tensor.matmul(aux[:, 3, 0:P], probs_t[:, n % 2, k, :],
                                          v_tok[:, k, P * hd:P * (hd + 1)], start=(k == 0), stop=(k == qb))
                mm.then_inc(pv_done, 1)

            def channel_sum(src, n):
                claim([2], *((ln_centered, 2) if n == 0 else (ln_var, 1)))
                for kt in range(KT):
                    mm = nc.tensor.matmul(aux[:, 2, 0:S], mean_w[:, :], src[:, kt, :], start=(kt == 0),
                                          stop=(kt == KT - 1))
                mm.then_inc(ln_sum, 1)

            def scores2(n):
                if n == 0:
                    pe.wait_ge(qk_kept, 12)
                for j in range(2):
                    bank = 2 * (n % 2) + j
                    claim([bank], lw_ready, n + 1)
                    ps = slice(HD * j, HD * (j + 1))
                    nc.tensor.matmul(aux[:, bank, 0:S], k2_t[ps, n, 0:P], q2_t[ps, n, 0:S], start=True, stop=False,
                                     skip_group_check=True)
                    mm = nc.tensor.matmul(aux[:, bank, S:ZC], k2_t[ps, n, P:S], q2_t[ps, n, P:S], start=False,
                                          stop=False, skip_group_check=True)
                mm.then_inc(z_made, 1)

            def suffixes(n):
                pe.wait_ge(sp_ready, n + 1)
                for j in range(2):
                    bank, sp_ = 2 * (n % 2) + j, w2_t[:, 2 * n + j, :]
                    nc.tensor.matmul(aux[:, bank, 0:S], neg_tri[:, :], sp_[:, 0:S], start=False, stop=False,
                                     skip_group_check=True)
                    nc.tensor.matmul(aux[:, bank, P:S], neg_one[:, :], sp_[:, S:ZC], start=False, stop=False,
                                     skip_group_check=True)
                    mm = nc.tensor.matmul(aux[:, bank, S:ZC], neg_tri[:, :], sp_[:, S:ZC], start=False, stop=True,
                                          skip_group_check=True)
                mm.then_inc(sfx_done, 1)

            def attend2(n):
                pe.wait_ge(w2_ready, n + 1)
                claim([n], o2_lo, n + 1)
                for j in range(2):
                    ps = slice(HD * j, HD * (j + 1))
                    c0 = HD * (2 * n + j)
                    nc.tensor.matmul(aux[ps, n, 0:S], v2[:, 0, c0:c0 + HD], w2_t[:, 2 * n + j, 0:S], start=True,
                                     stop=False, skip_group_check=True)
                    mm = nc.tensor.matmul(aux[ps, n, P:S], v2[:, 1, c0:c0 + HD], w2_t[:, 2 * n + j, S:ZC],
                                          start=False, stop=True, skip_group_check=True)
                mm.then_inc(pv2_done, 1)

            def lru_gates(ct):
                pe.wait_ge(u2_ready, TAPS2 * CT2)
                pe.wait_ge(lru_w_in, 64)
                bank = LRU_BANK[ct]
                claim([bank], ri_kept, 2 * ct + 2)
                nc.tensor.matmul(aux[:, bank, 0:S], wr_g[:, ct, :], u2[:, ct, :], start=True, stop=True)
                nc.tensor.matmul(aux[:, bank, S:2 * S], wi_g[:, ct, :], u2[:, ct, :], start=True, stop=True)\
                    .then_inc(ri_made, 1)

            def wait_stationary(c, k1):
                kind, i = chunks[c][:2]
                if kind == "pc":
                    pe.wait_ge(c_lo_ready, k1 // 4)
                elif kind == "pa":
                    pe.wait_ge(a_lo, k1 // 2)
                elif kind == "res" and i < 2:
                    pe.wait_ge(mix_lo, k1 // 2)
                elif kind == "res" and i < 4:
                    pe.wait_ge(ff_lo, k1 // 2)
                elif kind == "res" and i < 6:
                    if k1 > CT2:
                        pe.wait_ge(lru_lo, 1)
                    else:
                        pe.wait_ge(o2_lo, 4)
                elif kind == "res":
                    pe.wait_ge(up_lo, k1 // 2)
                else:
                    st = {"ff": 1, "up": 3}.get(kind, 0 if c <= number["g", 3] else 2)
                    pe.wait_ge(stage_lo, 8 * st + k1)

            def parts(c):
                kind, i = chunks[c][:2]
                if kind == "pa" or (kind == "res" and i in (0, 1, 4, 5)):
                    return c_hi, c_lo
                if kind == "res":
                    return m_hi, m_lo
                return h_hi, h_lo

            def halfway(s):
                for i in range(4):
                    if s == end["u", i] + 1:
                        turn_glu(i, 1)
                for kind, i in QK:
                    if s == end[kind, i] + 1:
                        turn_qk(kind, i, 0)
                for n in range(NA):
                    if s == ATT[n] + 3:
                        attend(n)
                if s == end["pc", 1]:
                    turn_mix((2, 3))
                for i in (1, 3, 5):
                    if s == end["res", i]:
                        pe.wait_ge(added, 2 * i + 2)
                        stage(i // 2 + 1, (2, 3))
                if s == B + 3:
                    turn2(x2_tok, 1, x2_kept, x2_turned, x2_in)
                if s == B + 5:
                    for ct in range(3):
                        lru_gates(ct)
                if s == B + 8:
                    scores2(0)
                if s == B + 9:
                    suffixes(0)
                    scores2(1)
                if s == B + 10:
                    suffixes(2)
                    scores2(3)
                if s == B + 11:
                    pe.wait_ge(v_kept, 6)
                    attend2(0)
                    attend2(1)

            def turn_mix(pairs):
                pe.wait_ge(branch_sum, 2 * (pairs[0] // 2) + 2)
                for g in pairs:
                    claim([STAGE[g]], mix_lo, g + 1)
                    turn_pair(gates, g, STAGE[g]).then_inc(mix_turned, 1)

            def turn2(src, t, s_in, s_out, s_kept):
                pe.wait_ge(s_in, t + 1)
                claim([TURN2_BANK[t]], s_kept, t + 1)
                turn_four(src[:, t, :], TURN2_BANK[t]).then_inc(s_out, 1)

            def after(s):
                for i in range(4):
                    if s == end["u", i]:
                        turn_glu(i, 0)
                for kind, i in QK:
                    if s == end[kind, i] + 1:
                        turn_qk(kind, i, 1)
                for n in range(NA):
                    if s == ATT[n] + 2:
                        turn_probs(n)
                for n in range(NA):
                    if s == ATT[n]:
                        scores(n)
                if s == LN:
                    pe.wait_ge(conv_done, CONV_OPS)
                    channel_sum(conv, 0)
                if s == LN + 1:
                    pe.wait_ge(ln_sq, 2)
                    channel_sum(c_sq, 1)
                if s in a_steps:
                    for g in a_steps[s]:
                        pe.wait_ge(a_scaled, 2 * (g // 2) + 2)
                        claim([g % 2], a_lo, g + 1)
                        turn_pair(a_tok, g, g % 2).then_inc(a_turned, 1)
                if s == end["pc", 0]:
                    turn_mix((0, 1))
                for i in (0, 2, 4):
                    if s == end["res", i]:
                        pe.wait_ge(added, 2 * i + 2)
                        stage(i // 2 + 1, (0, 1))
                for i in range(FF // 256):
                    if s == end["ff", i]:
                        pe.wait_ge(ff_made, 2 * i + 2)
                        claim([i % 2], ff_lo, i + 1)
                        for j in range(2):
                            for t in range(NT):
                                mm = turn(aux[:, i % 2, 256 * j + P * t:256 * j + P * (t + 1)],
                                          ff_m[:, t, P * j:P * (j + 1)])
                        mm.then_inc(ff_turned, 1)
                for i in range(FF2 // CW):
                    if s == end["up", i]:
                        pe.wait_ge(up_sq, 2 * i + 2)
                        for j in range(2):
                            claim([j], up_lo, 2 * i + j + 1)
                            turn_pair(tok, j, j).then_inc(up_turned, 1)
                if s == B + 2:
                    turn2(x2_tok, 0, x2_kept, x2_turned, x2_in)
                if s == B + 5:
                    lru_gates(3)
                if s == B + 8:
                    turn2(g2_tok, 0, g2_kept, g2_turned, g2_in)
                    turn2(g2_tok, 1, g2_kept, g2_turned, g2_in)
                if s == B + 9:
                    suffixes(1)
                    scores2(2)
                if s == B + 10:
                    suffixes(3)
                if s == B + 11:
                    attend2(2)
                    attend2(3)

            pe.wait_ge(ident_ready, 1)
            pe.wait_ge(vecs_loaded, 16)
            claim([2], vec_ready, 1)
            for kt in range(KT):
                mm = nc.tensor.transpose(aux[:, 2, VROWS * kt:VROWS * (kt + 1)], vecs[:, P * kt:P * (kt + 1)],
                                         ident[0:VROWS, 0:VROWS])
            mm.then_inc(vec_turned, 1)
            for t in range(NT):
                pe.wait_ge(x_loaded[t], 16)
            stage(0, range(4))
            pe.wait_ge(consts_loaded, 32)
            pe.wait_ge(zeros_ready, 5)
            claim([2], rel_kept, 1)
            nc.tensor.matmul(aux[0:H, 2, 0:RELS], rel_aug[:, :], onehot[:, :], start=True, stop=True).then_inc(rel_made, 1)

            for s, (c, k0, nk, is_first, is_last) in enumerate(units):
                if is_first and c >= 2:
                    pe.wait_ge(*freed_by(c - 2))
                wait_stationary(c, k0 + nk)
                pe.wait_ge(w_hi_ready, s + 1)
                pe.wait_ge(w_lo_pool if on_pool(s) else w_lo_dve, low_no[s])
                hi, lo = parts(c)
                slot = s % SPLIT
                for j in range(nk):
                    for t in range(NT):
                        o = acc_of(c, t)
                        x_h = hi[:, k0 + j, P * t:P * (t + 1)]
                        x_l = lo[:, k0 + j, P * t:P * (t + 1)]
                        begin_ = is_first and j == 0
                        end_ = is_last and j == nk - 1
                        nc.tensor.matmul(o, x_h, w_hi[:, slot, j, :], start=begin_, stop=False)
                        nc.tensor.matmul(o, x_h, w_lo[:, slot, j, :], start=False, stop=False)
                        mm = nc.tensor.matmul(o, x_l, w_hi[:, slot, j, :], start=False, stop=end_)
                    if j == nk - 1:
                        mm.then_inc(unit_done, 1)
                    if j == 1:
                        halfway(s)
                after(s)


def t5_one_hot():
    e = np.zeros((VROWS, RELS), np.float32)
    exact = BUCKETS // 2
    for m in range(RELS):
        n = 255 - m
        if n < 0:
            e[BUCKETS, m] = 1.0
            continue
        b = n
        if n >= exact:
            b = min(exact + int(math.log(n / exact) / math.log(MAX_DIST / exact) * (BUCKETS - exact)), BUCKETS - 1)
        e[b, m] = 1.0
    return e


def small_vectors(g):
    v = np.zeros((VROWS, D), np.float32)
    rows = [(R_CONV_W, g["conv_w"][0]), (R_CONV_B, g["conv_b"]), (R_LN_W, g["conv_ln_w"]), (R_LN_B, g["conv_ln_b"]),
            (R_NORM[0], g["attn_norm_w"]), (R_NORM[1], g["ffn_norm_w"]), (R_NORM[2], g["norm1_g_2"]),
            (R_NORM[3], g["norm2_g_2"]), (R_CONV2_W, g["conv_w_2"][0]), (R_CONV2_B, g["conv_b_2"]),
            (R_RG, g["b_rg_2"]), (R_IG, g["b_ig_2"]), (R_LAMBDA, g["lru_lambda_2"]),
            (R_Q, np.concatenate([g["q_norm_w"]] * 2, 1)), (R_K, np.concatenate([g["k_norm_w"]] * 2, 1)),
            (R_SUB, g["subln_w"]), (R_Q2, np.concatenate([g["q_norm_g_2"]] * 2, 1)),
            (R_K2, np.concatenate([g["k_norm_g_2"]] * 2, 1))]
    for r, x in rows:
        v[r:r + x.shape[0], 0:x.shape[1]] = x
    return v


DIRECT = ["x", "lam_q1", "lam_k1", "lam_q2", "lam_k2", "gate_b", "rel_bias", "w_in", "w_proj_attn", "w_proj_conv",
          "w_out", "w_gate_up", "w_down", "w_in_2", "w_rg_2", "w_ig_2", "w_out_2", "w_up_2", "w_down_2"]
WEIGHTS = ["w_in", "w_proj_attn", "w_proj_conv", "w_out", "w_gate_up", "w_down", "w_in_2", "w_out_2", "w_up_2",
           "w_down_2"]


def kernel(**inputs):
    import concourse.bacc as bacc
    from concourse.bass_utils import run_bass_kernel_spmd

    g = {k: np.ascontiguousarray(v) for k, v in inputs.items()}
    arrays = {f"{k}_dram": g[k] for k in DIRECT}
    arrays["vectors_dram"] = small_vectors(g)
    arrays["bucket_onehot_dram"] = t5_one_hot()
    nc = bacc.Bacc("TRN2", target_bir_lowering=False, num_devices=1)
    aps = {k[:-5]: nc.dram_tensor(k, v.shape, F32, kind="ExternalInput").ap() for k, v in arrays.items()}
    for k in WEIGHTS:
        aps[k] = aps[k].rearrange("o k n -> (o k) n")
    out = nc.dram_tensor("out_dram", (1, S, D), F32, kind="ExternalOutput").ap()
    build(nc, aps, out)
    r = run_bass_kernel_spmd(nc, [arrays], core_ids=[0])
    return r.results[0]["out_dram"]
```

```python
import math
from contextlib import ExitStack

import numpy as np

import concourse.bass as bass
from concourse import mybir

F32 = mybir.dt.float32
F32R = mybir.dt.float32r
ALU = mybir.AluOpType
ACT = mybir.ActivationFunctionType
AX = mybir.AxisListType

P = 128
D = 1024
S = 256
NT = S // P
EPS = 1e-6
KT = D // P
CW = 512
UK = 4

H = 8
HD = 64
SC = HD ** -0.5
TAPS = 31
PAD = TAPS - 1
FF = 2816
FK = FF // P
BUCKETS, MAX_DIST = 32, 128
MASKED = -1e30
LAM_INIT = 0.8 - 0.6 * math.exp(-0.3 * 0)
RELS = 384

W2 = 512
CT2 = W2 // P
IN2 = 3 * W2 + 2 * W2
TAPS2 = 4
FF2 = 4 * D
FK2 = FF2 // P
LRU_C = 8.0
EXP_LN_TABLES = 6
ZC = 384

R_CONV_W, R_CONV_B, R_LN_W, R_LN_B = 0, 31, 32, 33
R_NORM = (34, 35, 36, 37)
R_CONV2_W, R_CONV2_B, R_RG, R_IG, R_LAMBDA = 38, 42, 43, 44, 45
R_Q, R_K, R_SUB, R_Q2, R_K2 = 46, 47, 48, 49, 50
VROWS = 64


def weight_chunks(w):
    half = [0, UK]
    q = lambda g: ("q", g, w["w_in"], CW * g, None, half, KT)
    k = lambda g: ("k", g, w["w_in"], D + CW * g, None, half, KT)
    v = lambda g: ("v", g, w["w_in"], 2 * D + CW * g, None, half, KT)
    u = lambda i: ("u", i, w["w_in"], 3 * D + 256 * i, D, half, KT)
    out = [u(0), q(0), k(0), u(1), v(0), q(1), k(1), u(2), v(1), u(3)]
    out += [("g", i, w["w_in"], 5 * D + CW * i, None, half, KT) for i in range(4)]
    out += [("pa", i, w["w_proj_attn"], CW * i, None, half, KT) for i in range(2)]
    out += [("pc", i, w["w_proj_conv"], CW * i, None, half, KT) for i in range(2)]
    out += [("res", i, w["w_out"], CW * i, None, half, KT) for i in range(2)]
    out += [("ff", i, w["w_gate_up"], 256 * i, FF, half, KT) for i in range(FF // 256)]
    out += [("res", 2 + i, w["w_down"], CW * i, None, list(range(0, FK, UK)), FK) for i in range(2)]
    out += [("x2", 0, w["w_in_2"], 3 * W2, None, half, KT), ("q", 2, w["w_in_2"], 0, None, half, KT),
            ("k", 2, w["w_in_2"], W2, None, half, KT), ("g2", 0, w["w_in_2"], 4 * W2, None, half, KT),
            ("v", 2, w["w_in_2"], 2 * W2, None, half, KT)]
    out += [("res", 4 + i, w["w_out_2"], CW * i, None, [UK, 0], KT) for i in range(2)]
    out += [("up", i, w["w_up_2"], CW * i, None, half, KT) for i in range(FF2 // CW)]
    out += [("res", 6 + i, w["w_down_2"], CW * i, None, list(range(0, FK2, UK)), FK2) for i in range(2)]
    return out


def build(nc, a, out):
    chunks = weight_chunks(a)
    units = []
    for c, ch in enumerate(chunks):
        for n, k0 in enumerate(ch[5]):
            units.append((c, k0, min(UK, ch[6] - k0), n == 0, n == len(ch[5]) - 1))
    u0 = next(u for u, x in enumerate(units) if chunks[x[0]][:2] == ("res", 4))
    units[u0 + 1], units[u0 + 2] = units[u0 + 2], units[u0 + 1]
    first = [next(u for u, x in enumerate(units) if x[0] == c) for c in range(len(chunks))]
    last = [max(u for u, x in enumerate(units) if x[0] == c) for c in range(len(chunks))]
    NU = len(units)
    number = {(ch[0], ch[1]): c for c, ch in enumerate(chunks)}
    end = {key: last[c] + 1 for key, c in number.items()}
    begin = {key: first[c] for key, c in number.items()}
    STAGE = [0, 1, 2, 0]
    ended = {last[c] + 1: (chunks[c][0], chunks[c][1], c) for c in range(len(chunks))}

    RAW, SPLIT = 3, 3
    LEAD = 2

    raw_value = []
    for u, (c, *_) in enumerate(units):
        raw_value.append((raw_value[u - RAW] if u >= RAW else 0) + (16 if chunks[c][4] is None else 32))

    B = begin["x2", 0]

    def on_pool(u):
        return 7 <= u <= 33 or B + 8 <= u <= B + 13
    low_no = []
    counts = {True: 0, False: 0}
    for u in range(NU):
        counts[on_pool(u)] += 1
        low_no.append(counts[on_pool(u)])

    ATT = [*range(8, 24)]
    NA = 2 * H
    CONV_OPS = TAPS * KT
    quota = {}
    done_ops = 0
    avail = {}
    for i in range(4):
        avail[i] = end["u", i] + 2
    for s in range(NU + 1):
        n = 10 if s < 10 else 8 if s < 18 else 12
        pairs = sum(1 for i in range(4) if avail[i] <= s)
        quota[s] = max(0, min(n, 2 * TAPS * pairs - done_ops))
        done_ops += quota[s]
    conv_last = max(s for s in range(NU) if quota[s])
    total = np.cumsum([quota[s] for s in range(NU)])
    ADDED = [int(np.searchsorted(total, 2 * TAPS * (pair + 1))) + 1 for pair in range(3)]
    LN = conv_last

    with ExitStack() as ctx:
        cursor = [(nc.sbuf_base + 31) // 32 * 32]

        def place(name, shape, dt=F32, at=None):
            size = int(np.prod(shape[1:])) * 4
            if at is None:
                at = cursor[0]
                cursor[0] += (size + 31) // 32 * 32
            return nc.alloc_sbuf_tensor_at(name, shape, dt, offset=at), at

        def sb(name, shape, dt=F32, at=None):
            return place(name, shape, dt, at)[0]

        def sem(name):
            return ctx.enter_context(nc.semaphore(name))

        raw = sb("raw", [P, RAW, UK, CW])
        w_hi = sb("w_hi", [P, SPLIT, UK, CW], F32R)
        w_lo = sb("w_lo", [P, SPLIT, UK, CW], F32R)
        h_hi = sb("h_hi", [P, KT, S], F32R)
        h_lo, at = place("h_lo", [P, KT, S], F32R)
        centered_sq = sb("centered_sq", [P, KT, S], at=at)
        y_hi = sb("y_hi", [P, KT, S], F32R)
        y_lo = sb("y_lo", [P, KT, S], F32R)
        conv, at = place("conv", [P, KT, S])
        x_res = sb("x_res", [P, NT, D], at=at)
        vec_t = sb("vec_t", [P, KT, VROWS])
        ident = sb("ident", [P, P])
        mean_w = sb("mean_w", [P, P])
        rstd = sb("rstd", [P, 4, NT])
        ss = sb("ss", [P, 4, 2, NT])
        ms = sb("ms", [P, 4, NT])
        nhalf = sb("nhalf", [P, 16])
        small = sb("small", [P, 64])
        qk_ss = sb("qk_ss", [P, 16])
        qk_r = sb("qk_r", [P, 16])
        lam_v = sb("lam_v", [P, 4, HD])
        gains = sb("gains", [P, 4])
        qk_c = sb("qk_c", [P, 16])
        tok = sb("tok", [P, NT, CW])
        junk_a, junk_l = sb("junk_a", [P, P]), sb("junk_l", [P, 2, HD])
        junk = sb("junk", [P, CW])
        region = cursor[0]
        gates, x_at = place("gates", [P, NT, 2 * D])
        x_in = sb("x_in", [P, NT, D], at=x_at)
        vecs = sb("vecs", [VROWS, D], at=x_at + 4 * NT * D)
        onehot = sb("onehot", [VROWS, RELS], at=x_at + 4 * NT * D + 4 * D)
        rel_aug = sb("rel_aug", [VROWS, H], at=x_at + 4 * NT * D + 4 * D + 4 * RELS)
        rel_row = sb("rel_row", [H, RELS], at=x_at + 4 * NT * D + 4 * D + 4 * RELS + 64)
        q_t = sb("q_t", [P, H, S])
        k_t = sb("k_t", [P, H, S])
        v_tok = sb("v_tok", [P, NT, D])
        glu_t = sb("glu_t", [P, KT, PAD + S])
        a_tok = sb("a_tok", [P, NT, D])
        bias = sb("bias", [P, H, S])
        probs = sb("probs", [P, 2, 2, S])
        probs_t = sb("probs_t", [P, 2, 2, P])
        gate_bias = sb("gate_bias", [P, 2, CW])
        glu, at = place("glu", [P, NT, 256])
        gate_bias_2 = sb("gate_bias_2", [P, 2, CW], at=at)
        sig = sb("sig", [P, NT, 256])
        st_max = sb("st_max", [P, NA, 2])
        st_sum = sb("st_sum", [P, NA, 2])
        st_rec = sb("st_rec", [P, NA, 2])
        st_mix = sb("st_mix", [P, NA])
        a_ss = sb("a_ss", [P, NA])
        a_ms = sb("a_ms", [P, NA])
        a_r = sb("a_r", [P, NA])
        ln_r, at = place("ln_r", [P, S])
        conv_sum = sb("conv_sum", [P, S], at=at)
        assert cursor[0] <= nc.sbuf_usable_end, cursor[0]
        cursor[0] = region
        m_hi = sb("m_hi", [P, FK2, S], F32R)
        m_lo = sb("m_lo", [P, FK2, S], F32R)
        assert cursor[0] <= nc.sbuf_usable_end, cursor[0]
        ff_m = sb("ff_m", [P, NT, 256])
        ff_s = sb("ff_s", [P, NT, 256])
        mask = sb("mask", [P, ZC])
        neg_mask = sb("neg_mask", [P, ZC])
        neg_tri = sb("neg_tri", [P, P])
        neg_one = sb("neg_one", [P, P])
        coef = sb("coef", [P, CT2])
        sp_a = sb("sp_a", [P, 8, CT2])
        wr_g = sb("wr_g", [P, CT2, P])
        wi_g = sb("wi_g", [P, CT2, P])
        assert cursor[0] <= nc.sbuf_usable_end, cursor[0]
        cursor[0] = region
        q2_t = sb("q2_t", [P, CT2, S])
        k2_t = sb("k2_t", [P, CT2, S])
        v2 = sb("v2", [P, NT, W2])
        x2_tok, at = place("x2_tok", [P, NT, W2])
        decay_gate = sb("decay_gate", [P, CT2, S], at=at)
        g2_tok = sb("g2_tok", [P, NT, W2])
        x2_t = sb("x2_t", [P, CT2, TAPS2 - 1 + S])
        lru_u = sb("lru_u", [P, CT2, S])
        in_gate = sb("in_gate", [P, CT2, S])
        decay = sb("decay", [P, CT2, S])
        lru_tmp = sb("lru_tmp", [P, CT2, S])
        gelu_t = sb("gelu_t", [P, CT2, S])
        soft = sb("soft", [P, 2, ZC])
        soft2 = sb("soft2", [P, 2, ZC])
        w2_t = sb("w2_t", [P, 8, ZC])
        assert cursor[0] <= region + 2 * 4 * FK2 * S, cursor[0]

        acc = ctx.enter_context(nc.psum_tensor("acc", [P, 2, NT, CW], F32))
        aux = ctx.enter_context(nc.psum_tensor("aux", [P, 4, CW], F32))
        rel_dram = nc.dram_tensor("rel_scratch", [H * P * RELS], F32, kind="Internal")

        raw_in = [sem(f"raw_in{i}") for i in range(RAW)]
        x_loaded = [sem(f"x_loaded{t}") for t in range(NT)]
        vecs_loaded, consts_loaded, lam_loaded = sem("vecs_loaded"), sem("consts_loaded"), sem("lam_loaded")
        rel_stored, bias_loaded = sem("rel_stored"), sem("bias_loaded")
        x_reloaded = sem("x_reloaded")
        gate_bias_in = [sem("gate_bias_in0"), sem("gate_bias_in1")]
        lru_w_in = sem("lru_w_in")
        stored = sem("stored")
        w_hi_ready, w_lo_dve, w_lo_pool, unit_done = (sem("w_hi_ready"), sem("w_lo_dve"), sem("w_lo_pool"),
                                                      sem("unit_done"))
        ident_ready, zeros_ready, pool_consts = sem("ident_ready"), sem("zeros_ready"), sem("pool_consts")
        vec_turned, vec_ready = sem("vec_turned"), sem("vec_ready")
        rel_made, rel_kept, lam_sums, lam_exp, lam_ready = (sem("rel_made"), sem("rel_kept"), sem("lam_sums"),
                                                           sem("lam_exp"), sem("lam_ready"))
        stage_turned, stage_hi, stage_lo = sem("stage_turned"), sem("stage_hi"), sem("stage_lo")
        squares, mean_sq, rstd_ready, ms_parts = sem("squares"), sem("mean_sq"), sem("rstd_ready"), sem("ms_parts")
        sig_made, glu_made, glu_turned, glu_kept = sem("sig_made"), sem("glu_made"), sem("glu_turned"), sem("glu_kept")
        qk_sq, qk_sum, qk_pow, qk_coef, qk_normed = (sem("qk_sq"), sem("qk_sum"), sem("qk_pow"), sem("qk_coef"),
                                                     sem("qk_normed"))
        qk_turned, qk_kept, v_kept = sem("qk_turned"), sem("qk_kept"), sem("v_kept")
        conv_done, conv_added, sq_added = sem("conv_done"), sem("conv_added"), sem("sq_added")
        scored, biased, maxed, exped, summed, mixed = (sem("scored"), sem("biased"), sem("maxed"),
                                                               sem("exped"), sem("summed"), sem("mixed"))
        probs_turned, probs_kept, pv_done, a_kept, a_mean, a_pow, a_scaled = (
            sem("probs_turned"), sem("probs_kept"), sem("pv_done"), sem("a_kept"), sem("a_mean"), sem("a_pow"),
            sem("a_scaled"))
        a_turned, a_hi, a_lo = sem("a_turned"), sem("a_hi"), sem("a_lo")
        ln_sum, ln_centered, ln_sq, ln_var, ln_sd, ln_rec, ln_y, ln_act, conv_hi_ready, conv_lo_ready = (
            sem("ln_sum"), sem("ln_centered"), sem("ln_sq"), sem("ln_var"), sem("ln_sd"), sem("ln_rec"), sem("ln_y"),
            sem("ln_act"), sem("conv_hi_ready"), sem("conv_lo_ready"))
        gate_kept, gate_biased, gated, branch, branch_sum = (sem("gate_kept"), sem("gate_biased"), sem("gated"),
                                                             sem("branch"), sem("branch_sum"))
        mix_turned, mix_hi, mix_lo = sem("mix_turned"), sem("mix_hi"), sem("mix_lo")
        added = sem("added")
        sp_made, a_squared, qk_reduced, lru_out = sem("sp_made"), sem("a_squared"), sem("qk_reduced"), sem("lru_out")
        ff_act, ff_made, ff_turned, ff_hi, ff_lo = (sem("ff_act"), sem("ff_made"), sem("ff_turned"), sem("ff_hi"),
                                                    sem("ff_lo"))
        up_act, up_sq, up_turned, up_hi, up_lo = (sem("up_act"), sem("up_sq"), sem("up_turned"), sem("up_hi"),
                                                  sem("up_lo"))
        sp_act, sp_dve, coef_ready = sem("sp_act"), sem("sp_dve"), sem("coef_ready")
        x2_kept, x2_turned, x2_in, g2_kept, g2_turned, g2_in = (sem("x2_kept"), sem("x2_turned"), sem("x2_in"),
                                                               sem("g2_kept"), sem("g2_turned"), sem("g2_in"))
        pads_ready, u2_ready, ri_made, ri_kept = sem("pads_ready"), sem("u2_ready"), sem("ri_made"), sem("ri_kept")
        lru_act, lru_dve, lru_root, iu_ready, lru_hi, lru_lo = (sem("lru_act"), sem("lru_dve"), sem("lru_root"),
                                                                sem("iu_ready"), sem("lru_hi"), sem("lru_lo"))
        z_made, z_act, sp_ready, sfx_done, lw_ready, w2_ready, pv2_done, o2_hi, o2_lo = (
            sem("z_made"), sem("z_act"), sem("sp_ready"), sem("sfx_done"), sem("lw_ready"), sem("w2_ready"),
            sem("pv2_done"), sem("o2_hi"), sem("o2_lo"))
        gains_ready = sem("gains_ready")

        def f(ap):
            return ap.bitcast(F32)

        def vcol(row, kt):
            return vec_t[:, kt, row:row + 1]

        def again(ap, times):
            return bass.AP(tensor=ap.tensor, offset=ap.offset, ap=[ap.ap[0], [0, times], *ap.ap[1:]])

        def spread(ap, width):
            return bass.AP(tensor=ap.tensor, offset=ap.offset, ap=[*ap.ap, [0, width]])

        def acc_of(c, t):
            return acc[:, c % 2, t, :]

        def stage_of(kind, i):
            return i // 2 + 1

        def freed_by(c):
            kind, i = chunks[c][:2]
            order = [ch[1] for ch in chunks if ch[0] == kind].index(i)
            if kind in "qk":
                return qk_normed, 2 * QK.index((kind, i)) + 2
            if kind == "g2":
                return g2_in, 2
            return {"u": glu_made, "v": v_kept, "g": gate_kept, "pc": branch, "pa": branch, "res": added,
                    "ff": ff_made, "x2": x2_kept, "up": up_act}[kind], \
                2 * (order + 1) + (4 if kind == "pc" else 0)

        QK = [(ch[0], ch[1]) for ch in chunks if ch[0] in ("q", "k")]
        a_steps = {24: (0, 1), 27: (2, 3)}

        def pair_banks(n):
            return slice(2 * (n % 2), 2 * (n % 2) + 2)

        LRU_BANK = [0, 1, 3, 0]

        NORMS = [end["res", i] for i in (1, 3, 5)]

        EARLY = begin["res", 0]

        block = ctx.enter_context(nc.Block())

        @block.sync
        def _(sp):
            x_rows = a["x"].rearrange("b (t p) d -> p (b t) d", p=P)
            for t in range(NT):
                sp.dma_start(x_in[:, t, :], x_rows[:, t, :]).then_inc(x_loaded[t], 16)
            for u, (c, k0, nk, _, _) in enumerate(units):
                _, _, w, col, pair, _, _ = chunks[c]
                n = w.shape[-1]
                if u >= RAW:
                    sp.wait_ge(w_hi_ready, u - RAW + 1)
                    sp.wait_ge(w_lo_pool if on_pool(u - RAW) else w_lo_dve, low_no[u - RAW])
                width = CW if pair is None else CW // 2
                for b in range(CW // width):
                    src = bass.AP(tensor=w.tensor, offset=w.offset + k0 * P * n + col + b * (pair or 0),
                                  ap=[[n, P], [P * n, nk], [1, width]])
                    sp.dma_start(raw[:, u % RAW, 0:nk, width * b:width * (b + 1)], src)\
                        .then_inc(raw_in[u % RAW], 16)
                if chunks[c][0] == "g" and chunks[c][1] in (0, 3) and k0 == 0:
                    i = chunks[c][1]
                    if i:
                        sp.wait_ge(glu_turned, 8)
                    gb = a["gate_b"]
                    src = bass.AP(tensor=gb.tensor, offset=gb.offset + (D if i else 0), ap=[[0, P], [1, D]])
                    dst = gate_bias_2 if i else gate_bias
                    sp.dma_start(dst.rearrange("p a b -> p (a b)"), src).then_inc(gate_bias_in[i // 3], 16)
                if u == begin["res", 0]:
                    sp.wait_ge(conv_lo_ready, 2)
                    sp.wait_ge(conv_hi_ready, 2)
                    sp.dma_start(x_res[:, :, :], x_rows).then_inc(x_reloaded, 16)
                if u == begin["res", 2]:
                    sp.wait_ge(pool_consts, 4)
                    for half in range(2):
                        for tile, w_g in ((wr_g, a["w_rg_2"]), (wi_g, a["w_ig_2"])):
                            ps = slice(HD * half, HD * half + HD)
                            src = w_g.rearrange("o (c b) i j -> b i (o c) j", b=2)[half]
                            sp.dma_start(tile[ps, :, ps], src).then_inc(lru_w_in, 16)
            o_rows = out.rearrange("b (t p) d -> p (b t) d", p=P)
            for i in range(2):
                for t in range(NT):
                    sp.wait_ge(added, 12 + 2 * i + t + 1)
                    cols = slice(CW * i, CW * (i + 1))
                    sp.dma_start(o_rows[:, t, cols], x_res[:, t, cols]).then_inc(stored, 16)
            sp.wait_ge(stored, 16 * 2 * NT)

        @block.gpsimd
        def _(pool):
            nc.gpsimd.memset(ident[:, :], 0.0).then_inc(zeros_ready, 1)
            pool.wait_ge(zeros_ready, 1)
            nc.gpsimd.affine_select(out=ident[:, :], in_=ident[:, :], compare_op=ALU.not_equal, fill=1.0, base=0,
                                    pattern=[[-1, P]], channel_multiplier=1).then_inc(ident_ready, 1)
            nc.gpsimd.memset(nhalf[:, :], -0.5).then_inc(zeros_ready, 1)
            nc.gpsimd.memset(mean_w[:, :], 1.0 / D).then_inc(zeros_ready, 1)
            nc.gpsimd.memset(rel_aug[:, :], 0.0).then_inc(zeros_ready, 1)
            pool.wait_ge(zeros_ready, 4)
            nc.gpsimd.memset(rel_aug[BUCKETS:BUCKETS + 1, :], MASKED).then_inc(zeros_ready, 1)
            pool.dma_start(rel_aug[0:BUCKETS, :], a["rel_bias"]).then_inc(consts_loaded, 16)
            pool.dma_start(onehot[:, :], a["bucket_onehot"]).then_inc(consts_loaded, 16)
            for i, name in enumerate(("lam_q1", "lam_k1", "lam_q2", "lam_k2")):
                lv = a[name]
                pool.dma_start(lam_v[:, i, :], bass.AP(tensor=lv.tensor, offset=lv.offset, ap=[[0, P], [1, HD]]))\
                    .then_inc(lam_loaded, 16)
            pool.wait_ge(zeros_ready, 5)
            nc.gpsimd.memset(glu_t[:, :, 0:PAD], 0.0).then_inc(zeros_ready, 1)

            def power(out_, in_, s_in, n_in, s_out):
                pool.wait_ge(s_in, n_in)
                nc.gpsimd.tensor_tensor(out_, in_, nhalf[:, 0:in_.shape[1]], ALU.pow).then_inc(s_out, 1)

            power(rstd[:, 0, :], ms[:, 0, :], mean_sq, 1, rstd_ready)
            pool.wait_ge(rel_kept, 1)
            pool.dma_start(rel_dram.ap().rearrange("(h q r) -> h q r", h=H, q=P), again(rel_row[:, :], P))\
                .then_inc(rel_stored, 16)
            pool.wait_ge(rel_stored, 16)
            pool.dma_start(bias[:, :, :], bass.AP(tensor=rel_dram, offset=P - 1,
                                                  ap=[[RELS - 1, P], [RELS * P, H], [1, S]])).then_inc(bias_loaded, 16)

            for s in range(NU):
                if s in ended:
                    kind, i, c = ended[s]
                    if kind in ("q", "k") and s != end["k", 0]:
                        j = QK.index((kind, i))
                        power(qk_r[:, :], qk_ss[:, :], qk_sum, j + 1, qk_pow)
                    if kind == "res" and i % 2 == 1 and i < 7:
                        st = stage_of(kind, i)
                        power(rstd[:, st, :], ms[:, st, :], mean_sq, st + 1, rstd_ready)
                for g in range(2):
                    if s == ATT[8 * g + 7] + 4:
                        power(a_r[:, 8 * g:8 * g + 8], a_ms[:, 8 * g:8 * g + 8], a_mean, g + 1, a_pow)
                for pair in range(3):
                    if s == ADDED[pair]:
                        pool.wait_ge(conv_done, 2 * TAPS * (pair + 1))
                        for ct in (2 * pair, 2 * pair + 1)[pair == 0:]:
                            if ct > 1:
                                pool.wait_ge(conv_added, ct - 1)
                            nc.gpsimd.tensor_tensor(conv_sum[:, :], conv[:, 0, :] if ct == 1 else conv_sum[:, :],
                                                    conv[:, ct, :], ALU.add).then_inc(conv_added, 1)
                if s == begin["ff", 3]:
                    pool.wait_ge(stage_lo, 16)
                    nc.gpsimd.memset(mask[:, :], 1.0).then_inc(zeros_ready, 1)
                    nc.gpsimd.memset(neg_mask[:, :], 0.0).then_inc(zeros_ready, 1)
                    nc.gpsimd.memset(neg_tri[:, :], -1.0).then_inc(zeros_ready, 1)
                    nc.gpsimd.memset(neg_one[:, :], -1.0).then_inc(pool_consts, 1)
                    nc.gpsimd.memset(wr_g[:, :, :], 0.0).then_inc(pool_consts, 1)
                    nc.gpsimd.memset(wi_g[:, :, :], 0.0).then_inc(pool_consts, 1)
                    pool.wait_ge(zeros_ready, 9)
                    for k0 in (0, 2 * P):
                        nc.gpsimd.affine_select(out=mask[:, k0:k0 + P], in_=mask[:, k0:k0 + P], compare_op=ALU.is_gt,
                                                fill=0.0, base=0, pattern=[[1, P]], channel_multiplier=-1)\
                            .then_inc(zeros_ready, 1)
                        nc.gpsimd.affine_select(out=neg_mask[:, k0:k0 + P], in_=neg_mask[:, k0:k0 + P],
                                                compare_op=ALU.is_gt, fill=MASKED, base=0, pattern=[[1, P]],
                                                channel_multiplier=-1).then_inc(zeros_ready, 1)
                    nc.gpsimd.affine_select(out=neg_tri[:, :], in_=neg_tri[:, :], compare_op=ALU.is_ge, fill=0.0,
                                            base=0, pattern=[[-1, P]], channel_multiplier=1).then_inc(pool_consts, 1)
                if s == B:
                    pool.wait_ge(unit_done, B)
                    nc.gpsimd.memset(x2_t[:, :, 0:TAPS2 - 1], 0.0).then_inc(pads_ready, 1)
                u = s + LEAD
                if u < NU and on_pool(u):
                    nk = units[u][2]
                    pool.wait_ge(w_hi_ready, u + 1)
                    nc.gpsimd.tensor_tensor(w_lo[:, u % SPLIT, 0:nk, :], raw[:, u % RAW, 0:nk, :],
                                            f(w_hi[:, u % SPLIT, 0:nk, :]), ALU.subtract).then_inc(w_lo_pool, 1)
                if s == end["k", 0]:
                    power(qk_r[:, :], qk_ss[:, :], qk_sum, QK.index(("k", 0)) + 1, qk_pow)

        @block.scalar
        def _(act):
            act.dma_start(vecs[:, :], a["vectors"]).then_inc(vecs_loaded, 16)

            def split_high(u):
                nk = units[u][2]
                act.wait_ge(raw_in[u % RAW], raw_value[u])
                if u >= SPLIT:
                    act.wait_ge(unit_done, u - SPLIT + 1)
                nc.scalar.activation(w_hi[:, u % SPLIT, 0:nk, :], raw[:, u % RAW, 0:nk, :], ACT.Copy)\
                    .then_inc(w_hi_ready, 1)

            def stage_high(st, g):
                act.wait_ge(stage_turned, 4 * st + g + 1)
                for j in range(2):
                    kt = 2 * g + j
                    nc.scalar.activation(h_hi[:, kt, :], aux[:, STAGE[g], 256 * j:256 * (j + 1)], ACT.Copy,
                                         scale=vcol(R_NORM[st], kt)).then_inc(stage_hi, 1)

            def pair_high(dst, g, bank, s_in, n_in, s_out, scale=1.0):
                act.wait_ge(s_in, n_in)
                nc.scalar.activation(dst[:, 2 * g:2 * g + 2, :], aux[:, bank, :].rearrange("p (a b) -> p a b", a=2),
                                     ACT.Copy, scale=scale).then_inc(s_out, 1)

            act.wait_ge(vec_turned, 1)
            nc.scalar.activation(vec_t[:, :, :], aux[:, 2, :].rearrange("p (a b) -> p a b", a=KT), ACT.Copy)\
                .then_inc(vec_ready, 1)
            act.wait_ge(vec_ready, 1)
            for half in range(2):
                stage_high(0, 2 * half)
                stage_high(0, 2 * half + 1)
                split_high(half)
            for t in range(NT):
                act.wait_ge(x_loaded[t], 16)
                for hf in range(2):
                    if t or hf:
                        act.wait_ge(squares, 2 * t + hf)
                    nc.scalar.activation(junk[:, :], x_in[:, t, CW * hf:CW * (hf + 1)], ACT.Square,
                                         accum_out=ss[:, 0, hf, t:t + 1]).then_inc(squares, 1)
            act.wait_ge(lam_sums, 2)
            nc.scalar.activation(small[:, 2:4], small[:, 0:2], ACT.Exp).then_inc(lam_exp, 1)
            nc.scalar.activation(gains[:, 0:1], vcol(R_SUB, 0), ACT.Copy, scale=1.0 - LAM_INIT).then_inc(gains_ready, 1)
            nc.scalar.activation(gains[:, 1:2], vcol(R_Q2, 0), ACT.Copy, scale=SC).then_inc(gains_ready, 1)

            def keep_qk(kind, i, t):
                j = QK.index((kind, i))
                act.wait_ge(qk_turned, 2 * j + t + 1)
                if i < 2:
                    dst = (q_t if kind == "q" else k_t)[:, 4 * i:4 * i + 4, P * t:P * (t + 1)]
                    gain = vcol(R_Q if kind == "q" else R_K, 0)
                else:
                    dst = (q2_t if kind == "q" else k2_t)[:, :, P * t:P * (t + 1)]
                    gain = gains[:, 1:2] if kind == "q" else vcol(R_K2, 0)
                    act.wait_ge(gains_ready, 2)
                nc.scalar.activation(dst, aux[:, 2, :].rearrange("p (a b) -> p a b", a=4), ACT.Copy, scale=gain)\
                    .then_inc(qk_kept, 1)

            def keep_glu(i, t):
                act.wait_ge(glu_turned, 2 * i + t + 1)
                nc.scalar.activation(glu_t[:, 2 * i:2 * i + 2, PAD + P * t:PAD + P * (t + 1)],
                                     aux[:, 2, 0:256].rearrange("p (a b) -> p a b", a=2), ACT.Copy).then_inc(glu_kept, 1)

            def softplus_parts(n):
                sf = (soft, soft2)[n % 2]
                act.wait_ge(z_made, n + 1)
                if n >= 2:
                    act.wait_ge(sp_made, n - 1)
                nc.scalar.activation(sf[:, :, :], aux[:, pair_banks(n), 0:ZC], ACT.Abs).then_inc(z_act, 1)
                if n == 0:
                    nc.scalar.add_instruction(mybir.InstLoadActFuncSet(name=nc.get_next_instruction_name(),
                                                                       act_func_set_id=EXP_LN_TABLES))
                act.wait_ge(z_act, 3 * n + 1)
                nc.scalar.activation(sf[:, :, :], sf[:, :, :], ACT.Exp, scale=-1.0).then_inc(z_act, 1)
                act.wait_ge(z_act, 3 * n + 2)
                nc.scalar.activation(sf[:, :, :], sf[:, :, :], ACT.Ln, bias=1.0).then_inc(z_act, 1)

            def weights2(n):
                act.wait_ge(lw_ready, n + 1)
                w2 = w2_t[:, 2 * n:2 * n + 2, :]
                nc.scalar.activation(w2, w2, ACT.Exp).then_inc(w2_ready, 1)

            def keep_turned2(dst, off, s_in, s_out):
                for t in range(NT):
                    act.wait_ge(s_in, t + 1)
                    src = acc_of(number["g2", 0], t) if dst is gelu_t else aux[:, 2, :]
                    nc.scalar.activation(dst[:, :, off + P * t:off + P * (t + 1)],
                                         src.rearrange("p (a b) -> p a b", a=4), ACT.Copy).then_inc(s_out, 1)

            for s in range(NU + 1):
                if s == 1:
                    act.wait_ge(rel_made, 1)
                    nc.scalar.activation(rel_row[:, :], aux[0:H, 2, 0:RELS], ACT.Copy).then_inc(rel_kept, 1)
                for i in range(FF // 256):
                    if s == end["ff", i] + 1:
                        pair_high(m_hi, i, i % 2, ff_turned, i + 1, ff_hi)
                for i in range(FF2 // CW):
                    if s == end["up", i] + 1:
                        for j in range(2):
                            pair_high(m_hi, 2 * i + j, j, up_turned, 2 * i + j + 1, up_hi)
                for at_, pairs in a_steps.items():
                    if s == at_ + 1:
                        for g in pairs:
                            if g == 0:
                                act.wait_ge(gains_ready, 1)
                            pair_high(y_hi, g, g % 2, a_turned, g + 1, a_hi, gains[:, 0:1])
                if s == end["pc", 0] + 1:
                    for g in range(2):
                        pair_high(y_hi, g, STAGE[g], mix_turned, g + 1, mix_hi)
                for i in (0, 2):
                    if s == end["res", i] + 1:
                        stage_high(i // 2 + 1, 0)
                        stage_high(i // 2 + 1, 1)
                for i in range(4):
                    if s == end["u", i] + 2:
                        keep_glu(i, 1)
                for kind, i in QK:
                    if s == end[kind, i] + 2:
                        keep_qk(kind, i, 0 if i < 2 else 1)
                for n in range(NA):
                    if s == ATT[n] + 3:
                        act.wait_ge(probs_turned, n + 1)
                        if n >= 2:
                            act.wait_ge(pv_done, n - 1)
                        nk = n % 2 + 1
                        nc.scalar.activation(probs_t[:, n % 2, 0:nk, :],
                                             aux[:, 3, 0:P * nk].rearrange("p (a b) -> p a b", a=nk), ACT.Copy)\
                            .then_inc(probs_kept, 1)
                if (s < EARLY or s >= B) and s != LN + 3 and s not in NORMS and s + LEAD < NU:
                    split_high(s + LEAD)
                if s in ended:
                    kind, i, c = ended[s]
                    act.wait_ge(unit_done, last[c] + 1)
                    blk = 0 if c <= number["g", 3] else 2 if c >= number["x2", 0] else 1
                    if kind in ("u", "q", "k", "v", "x2", "g2"):
                        act.wait_ge(rstd_ready, blk + 1)
                    for t in range(NT):
                        r = rstd[:, blk, t:t + 1]
                        if kind == "u":
                            if i:
                                act.wait_ge(glu_made, 2 * (i - 1) + t + 1)
                            nc.scalar.activation(sig[:, t, :], acc_of(c, t)[:, 256:512], ACT.Sigmoid, scale=r)\
                                .then_inc(sig_made, 1)
                        if kind in ("q", "k"):
                            j = QK.index((kind, i))
                            if j:
                                act.wait_ge(qk_turned, 2 * (j - 1) + t + 1)
                            nc.scalar.activation(tok[:, t, :], acc_of(c, t), ACT.Square, scale=r).then_inc(qk_sq, 1)
                        if kind == "v":
                            dst = v_tok[:, t, CW * i:CW * (i + 1)] if i < 2 else v2[:, t, :]
                            nc.scalar.activation(dst, acc_of(c, t), ACT.Copy, scale=r).then_inc(v_kept, 1)
                        if kind == "x2":
                            nc.scalar.activation(x2_tok[:, t, :], acc_of(c, t), ACT.Copy, scale=r).then_inc(x2_kept, 1)
                        if kind == "g2":
                            nc.scalar.activation(g2_tok[:, t, :], acc_of(c, t), ACT.Gelu_apprx_tanh, scale=r)\
                                .then_inc(g2_kept, 1)
                        if kind == "g":
                            act.wait_ge(rstd_ready, 1)
                            nc.scalar.activation(gates[:, t, CW * i:CW * (i + 1)], acc_of(c, t), ACT.Copy, scale=r)\
                                .then_inc(gate_kept, 1)
                        if kind == "ff":
                            act.wait_ge(rstd_ready, 2)
                            if i:
                                act.wait_ge(ff_made, 2 * (i - 1) + t + 1)
                            nc.scalar.activation(ff_s[:, t, :], acc_of(c, t)[:, 0:256], ACT.Silu,
                                                 scale=rstd[:, 1, t:t + 1]).then_inc(ff_act, 1)
                        if kind == "up":
                            act.wait_ge(rstd_ready, 4)
                            if i:
                                act.wait_ge(up_turned, 2 * i)
                            nc.scalar.activation(tok[:, t, :], acc_of(c, t), ACT.Relu, scale=rstd[:, 3, t:t + 1])\
                                .then_inc(up_act, 1)
                        if kind == "res" and i < 6:
                            n = 4 + 2 * i + t
                            act.wait_ge(squares, n)
                            act.wait_ge(added, 2 * i + t + 1)
                            nc.scalar.activation(junk[:, :], x_res[:, t, CW * (i % 2):CW * (i % 2 + 1)], ACT.Square,
                                                 accum_out=ss[:, i // 2 + 1, i % 2, t:t + 1]).then_inc(squares, 1)
                for n in range(NA):
                    if s == ATT[n] + 1:
                        K = P * (n % 2 + 1)
                        act.wait_ge(maxed, n + 1)
                        for m in range(2):
                            pr = probs[:, n % 2, m, 0:K]
                            nc.scalar.activation(pr, pr, ACT.Exp, bias=st_max[:, n, m:m + 1],
                                                 accum_out=st_sum[:, n, m:m + 1]).then_inc(exped, 1)
                if EARLY <= s < B and s not in NORMS and s + LEAD < NU:
                    split_high(s + LEAD)
                for i in range(4):
                    if s == end["u", i] + 1:
                        keep_glu(i, 0)
                for kind, i in QK:
                    if i < 2 and s == end[kind, i] + 2:
                        keep_qk(kind, i, 1)
                    if i == 2 and s == end[kind, i] + 1:
                        keep_qk(kind, i, 0)
                for n in range(NA):
                    if s == ATT[n] + 3:
                        act.wait_ge(pv_done, n + 1)
                        hd, qb = n // 2, n % 2
                        if n:
                            act.wait_ge(a_squared, n)
                        nc.scalar.activation(junk_a[:, :], aux[:, 3, 0:P], ACT.Square,
                                             scale=st_rec[:, n, 0:1], accum_out=a_ss[:, n:n + 1]).then_inc(a_squared, 1)
                        nc.scalar.activation(a_tok[:, qb, P * hd:P * (hd + 1)], aux[:, 3, 0:P], ACT.Copy,
                                             scale=st_rec[:, n, 0:1]).then_inc(a_kept, 1)
                if s == end["pc", 1]:
                    for g in (2, 3):
                        pair_high(y_hi, g, STAGE[g], mix_turned, g + 1, mix_hi)
                if s == end["res", 4]:
                    stage_high(3, 0)
                    stage_high(3, 1)
                for i in (1, 3, 5):
                    if s == end["res", i]:
                        stage_high(i // 2 + 1, 2)
                        stage_high(i // 2 + 1, 3)
                        split_high(s + LEAD)
                if s == LN + 1:
                    for hf in range(2):
                        act.wait_ge(ln_centered, hf + 1)
                        nc.scalar.activation(centered_sq[:, 4 * hf:4 * hf + 4, :], conv[:, 4 * hf:4 * hf + 4, :], ACT.Square)\
                            .then_inc(ln_sq, 1)
                if s in (LN + 1, LN + 4):
                    for i in (0, 1) if s == LN + 1 else (2, 3):
                        act.wait_ge(gate_biased, i + 1)
                        gt = gates[:, :, CW * i:CW * (i + 1)]
                        nc.scalar.activation(gt, gt, ACT.Sigmoid).then_inc(gated, 1)
                if s == LN + 2:
                    act.wait_ge(ln_var, 1)
                    nc.scalar.activation(ln_r[:, :], ln_r[:, :], ACT.Sqrt).then_inc(ln_sd, 1)
                    for hf in range(2):
                        if hf:
                            split_high(s + 1 + LEAD)
                        act.wait_ge(ln_y, hf + 1)
                        for kt in range(4 * hf, 4 * hf + 4):
                            nc.scalar.activation(conv[:, kt, :], conv[:, kt, :], ACT.Silu, bias=vcol(R_LN_B, kt),
                                                 scale=vcol(R_LN_W, kt)).then_inc(ln_act, 1)
                        act.wait_ge(ln_act, 4 * hf + 4)
                        nc.scalar.activation(h_hi[:, 4 * hf:4 * hf + 4, :], conv[:, 4 * hf:4 * hf + 4, :], ACT.Copy)\
                            .then_inc(conv_hi_ready, 1)
                if s == begin["res", 2]:
                    nc.scalar.activation(sp_a[:, 0, :], vec_t[:, 0:CT2, R_LAMBDA], ACT.Abs).then_inc(sp_act, 1)
                    act.wait_ge(sp_act, 1)
                    nc.scalar.activation(sp_a[:, 1, :], sp_a[:, 0, :], ACT.Exp, scale=-1.0).then_inc(sp_act, 1)
                if s == B + 3:
                    keep_turned2(x2_t, TAPS2 - 1, x2_turned, x2_in)
                for ct in range(CT2):
                    if s == B + 6:
                        act.wait_ge(ri_made, ct + 1)
                        bank = LRU_BANK[ct]
                        nc.scalar.activation(decay_gate[:, ct, :], aux[:, bank, 0:256], ACT.Sigmoid, bias=vcol(R_RG, ct))\
                            .then_inc(ri_kept, 1)
                        nc.scalar.activation(in_gate[:, ct, :], aux[:, bank, 256:512], ACT.Sigmoid, bias=vcol(R_IG, ct))\
                            .then_inc(ri_kept, 1)
                if s == B + 6:
                    act.wait_ge(coef_ready, 1)
                    act.wait_ge(ri_kept, 2 * CT2)
                    for ct in range(CT2):
                        nc.scalar.activation(lru_tmp[:, ct, :], decay_gate[:, ct, :], ACT.Tanh, scale=coef[:, ct:ct + 1])\
                            .then_inc(lru_act, 1)
                    for ct in range(CT2):
                        nc.scalar.activation(decay[:, ct, :], decay_gate[:, ct, :], ACT.Exp, scale=coef[:, ct:ct + 1])\
                            .then_inc(lru_act, 1)
                if s == B + 7:
                    act.wait_ge(lru_dve, 2)
                    nc.scalar.activation(lru_tmp[:, :, :], lru_tmp[:, :, :], ACT.Sqrt, scale=-1.0).then_inc(lru_root, 1)
                if s == B + 8:
                    softplus_parts(0)
                if s == B + 9:
                    keep_turned2(gelu_t, 0, g2_turned, g2_in)
                    softplus_parts(1)
                    act.wait_ge(lru_out, 1)
                    nc.scalar.activation(y_hi[:, CT2:KT, :], lru_tmp[:, :, :], ACT.Copy).then_inc(lru_hi, 1)
                    weights2(0)
                if s == B + 10:
                    softplus_parts(2)
                    weights2(1)
                    softplus_parts(3)
                if s == B + 11:
                    weights2(2)
                    weights2(3)
                    for n in range(4):
                        act.wait_ge(pv2_done, n + 1)
                        nc.scalar.activation(y_hi[:, n, :], aux[:, n, 0:S], ACT.Copy).then_inc(o2_hi, 1)

        @block.vector
        def _(dve):
            def split_low(u):
                nk = units[u][2]
                dve.wait_ge(w_hi_ready, u + 1)
                nc.vector.tensor_tensor(w_lo[:, u % SPLIT, 0:nk, :], raw[:, u % RAW, 0:nk, :],
                                        f(w_hi[:, u % SPLIT, 0:nk, :]), ALU.subtract).then_inc(w_lo_dve, 1)

            def stage_low(st, g):
                for j in range(2):
                    kt = 2 * g + j
                    if j == 0:
                        dve.wait_ge(stage_hi, 8 * st + 2 * g + 2)
                    nc.vector.scalar_tensor_tensor(out=h_lo[:, kt, :], in0=aux[:, STAGE[g], 256 * j:256 * (j + 1)],
                                                   scalar=vcol(R_NORM[st], kt), in1=f(h_hi[:, kt, :]), op0=ALU.mult,
                                                   op1=ALU.subtract).then_inc(stage_lo, 1)

            def pair_low(hi, lo, g, bank, s_in, n_in, s_out):
                dve.wait_ge(s_in, n_in)
                nc.vector.tensor_tensor(lo[:, 2 * g:2 * g + 2, :], aux[:, bank, :].rearrange("p (a b) -> p a b", a=2),
                                        f(hi[:, 2 * g:2 * g + 2, :]), ALU.subtract).then_inc(s_out, 1)

            def mean_square(st):
                dve.wait_ge(squares, 4 * st + 4)
                nc.vector.tensor_tensor(ms[:, st, :], ss[:, st, 0, :], ss[:, st, 1, :], ALU.add).then_inc(ms_parts, 1)
                dve.wait_ge(ms_parts, st + 1)
                nc.vector.tensor_scalar(ms[:, st, :], ms[:, st, :], 1.0 / D, EPS, ALU.mult, ALU.add).then_inc(mean_sq, 1)

            def conv_step(o):
                pair, tap, ct = o // (2 * TAPS), o % (2 * TAPS) // 2, 2 * (o // (2 * TAPS)) + o % 2
                if o % (2 * TAPS) == 0:
                    dve.wait_ge(glu_kept, 2 * pair + 2)
                    if o == 0:
                        dve.wait_ge(zeros_ready, 6)
                if tap == 0:
                    nc.vector.tensor_scalar(conv[:, ct, :], glu_t[:, ct, 0:S], vcol(R_CONV_W, ct), vcol(R_CONV_B, ct),
                                            ALU.mult, ALU.add).then_inc(conv_done, 1)
                else:
                    dve.wait_ge(conv_done, o - 1)
                    nc.vector.scalar_tensor_tensor(out=conv[:, ct, :], in0=glu_t[:, ct, tap:tap + S],
                                                   scalar=vcol(R_CONV_W + tap, ct), in1=conv[:, ct, :], op0=ALU.mult,
                                                   op1=ALU.add).then_inc(conv_done, 1)

            def softplus_sum(n):
                dve.wait_ge(z_act, 3 * n + 3)
                if n == 0:
                    dve.wait_ge(pool_consts, 4)
                w2 = w2_t[:, 2 * n:2 * n + 2, :]
                nc.vector.scalar_tensor_tensor(out=w2, in0=aux[:, pair_banks(n), 0:ZC], scalar=0.0,
                                               in1=(soft, soft2)[n % 2][:, :, :], op0=ALU.max, op1=ALU.add)\
                    .then_inc(sp_made, 1)
                dve.wait_ge(sp_made, n + 1)
                nc.vector.tensor_tensor(w2, w2, again(mask[:, :], 2), ALU.mult).then_inc(sp_ready, 1)

            def log_weights(n):
                dve.wait_ge(sfx_done, n + 1)
                nc.vector.scalar_tensor_tensor(out=w2_t[:, 2 * n:2 * n + 2, :], in0=aux[:, pair_banks(n), 0:ZC],
                                               scalar=0.0, in1=again(neg_mask[:, :], 2), op0=ALU.min, op1=ALU.add)\
                    .then_inc(lw_ready, 1)

            def pv2_low(n):
                dve.wait_ge(o2_hi, n + 1)
                nc.vector.tensor_tensor(y_lo[:, n, :], aux[:, n, 0:S], f(y_hi[:, n, :]), ALU.subtract)\
                    .then_inc(o2_lo, 1)

            dve.wait_ge(vec_ready, 1)
            for half in range(2):
                stage_low(0, 2 * half)
                stage_low(0, 2 * half + 1)
                split_low(half)
            mean_square(0)
            dve.wait_ge(lam_loaded, 64)
            for i in range(2):
                nc.vector.tensor_tensor_reduce(junk_l[:, i, :], lam_v[:, 2 * i, :], lam_v[:, 2 * i + 1, :], 1.0, 0.0,
                                               ALU.mult, ALU.add, small[:, i:i + 1]).then_inc(lam_sums, 1)
            dve.wait_ge(lam_exp, 1)
            nc.vector.scalar_tensor_tensor(out=small[:, 4:5], in0=small[:, 3:4], scalar=LAM_INIT, in1=small[:, 2:3],
                                           op0=ALU.subtract, op1=ALU.subtract).then_inc(lam_ready, 1)
            taps_done = 0
            for s in range(NU + 1):
                for i in range(FF // 256):
                    if s == end["ff", i] + 1:
                        pair_low(m_hi, m_lo, i, i % 2, ff_hi, i + 1, ff_lo)
                for i in range(FF2 // CW):
                    if s == end["up", i] + 1:
                        for j in range(2):
                            pair_low(m_hi, m_lo, 2 * i + j, j, up_hi, 2 * i + j + 1, up_lo)
                for at_, pairs in a_steps.items():
                    if s == at_ + 1:
                        for g in pairs:
                            dve.wait_ge(a_hi, g + 1)
                            nc.vector.scalar_tensor_tensor(
                                out=y_lo[:, 2 * g:2 * g + 2, :], in0=aux[:, g % 2, :].rearrange("p (a b) -> p a b", a=2),
                                scalar=gains[:, 0:1], in1=f(y_hi[:, 2 * g:2 * g + 2, :]), op0=ALU.mult,
                                op1=ALU.subtract).then_inc(a_lo, 1)
                if s == end["pc", 0] + 1:
                    for g in range(2):
                        pair_low(y_hi, y_lo, g, STAGE[g], mix_hi, g + 1, mix_lo)
                for i in (0, 2):
                    if s == end["res", i] + 1:
                        stage_low(i // 2 + 1, 0)
                        stage_low(i // 2 + 1, 1)
                for n in range(NA):
                    if s == ATT[n] + 2:
                        K = P * (n % 2 + 1)
                        dve.wait_ge(exped, 2 * n + 2)
                        nc.vector.reciprocal(st_rec[:, n, :], st_sum[:, n, :]).then_inc(summed, 1)
                        dve.wait_ge(summed, 2 * n + 1)
                        if n == 0:
                            dve.wait_ge(lam_ready, 1)
                        nc.vector.scalar_tensor_tensor(out=st_mix[:, n:n + 1], in0=st_sum[:, n, 0:1],
                                                       scalar=small[:, 4:5], in1=st_rec[:, n, 1:2], op0=ALU.mult,
                                                       op1=ALU.mult).then_inc(summed, 1)
                for n in range(NA):
                    if s == ATT[n] + 2:
                        K = P * (n % 2 + 1)
                        dve.wait_ge(summed, 2 * n + 2)
                        nc.vector.scalar_tensor_tensor(out=probs[:, n % 2, 0, 0:K], in0=probs[:, n % 2, 1, 0:K],
                                                       scalar=st_mix[:, n:n + 1], in1=probs[:, n % 2, 0, 0:K],
                                                       op0=ALU.mult, op1=ALU.add).then_inc(mixed, 1)
                for g in range(2):
                    if s == ATT[8 * g + 7] + 4:
                        dve.wait_ge(a_squared, 8 * g + 8)
                        dve.wait_ge(a_kept, 8 * g + 8)
                        nc.vector.tensor_scalar(a_ms[:, 8 * g:8 * g + 8], a_ss[:, 8 * g:8 * g + 8], 1.0 / P, EPS,
                                                ALU.mult, ALU.add).then_inc(a_mean, 1)
                for _ in range(min(quota[s], 2)):
                    conv_step(taps_done)
                    taps_done += 1
                for n in range(NA):
                    if s == ATT[n] + 1:
                        hd, qb = n // 2, n % 2
                        K = P * (qb + 1)
                        dve.wait_ge(scored, n + 1)
                        if n == 0:
                            dve.wait_ge(bias_loaded, 16)
                        if n >= 2:
                            dve.wait_ge(probs_turned, n - 1)
                        pr = probs[:, n % 2, :, 0:K]
                        nc.vector.scalar_tensor_tensor(
                            out=pr, in0=aux[:, 0:2, 0:K], scalar=SC,
                            in1=again(bias[:, hd, S - K:S], 2), op0=ALU.mult, op1=ALU.add).then_inc(biased, 1)
                        dve.wait_ge(biased, n + 1)
                        nc.vector.tensor_reduce(st_max[:, n, :], pr, AX.X, ALU.max, negate=True).then_inc(maxed, 1)
                if s in ended:
                    kind, i, c = ended[s]
                    dve.wait_ge(unit_done, last[c] + 1)
                    blk = 0 if c <= number["g", 3] else 2 if c >= number["x2", 0] else 1
                    for t in range(NT):
                        r = rstd[:, blk, t:t + 1]
                        if kind == "u":
                            dve.wait_ge(sig_made, 2 * i + t + 1)
                            if i:
                                dve.wait_ge(glu_turned, 2 * (i - 1) + t + 1)
                            nc.vector.scalar_tensor_tensor(out=glu[:, t, :], in0=acc_of(c, t)[:, 0:256], scalar=r,
                                                           in1=sig[:, t, :], op0=ALU.mult, op1=ALU.mult)\
                                .then_inc(glu_made, 1)
                        if kind in ("q", "k"):
                            j = QK.index((kind, i))
                            dve.wait_ge(qk_sq, 2 * j + t + 1)
                            nc.vector.tensor_reduce(qk_ss[:, 8 * t:8 * t + 8],
                                                    tok[:, t, :].rearrange("p (a b) -> p a b", b=HD), AX.X, ALU.add)\
                                .then_inc(qk_reduced, 1)
                        if kind == "pc":
                            dve.wait_ge(gated, 2 + i + 1)
                            gt = gates[:, t, D + CW * i:D + CW * (i + 1)]
                            nc.vector.tensor_tensor(gt, acc_of(c, t), gt, ALU.mult).then_inc(branch, 1)
                        if kind == "pa":
                            dve.wait_ge(gated, i + 1)
                            gt = gates[:, t, CW * i:CW * (i + 1)]
                            nc.vector.tensor_tensor(gt, acc_of(c, t), gt, ALU.mult).then_inc(branch, 1)
                        if kind == "ff":
                            dve.wait_ge(ff_act, 2 * i + t + 1)
                            if i:
                                dve.wait_ge(ff_turned, i)
                            nc.vector.scalar_tensor_tensor(out=ff_m[:, t, :], in0=acc_of(c, t)[:, 256:512],
                                                           scalar=rstd[:, 1, t:t + 1], in1=ff_s[:, t, :], op0=ALU.mult,
                                                           op1=ALU.mult).then_inc(ff_made, 1)
                        if kind == "up":
                            dve.wait_ge(up_act, 2 * i + t + 1)
                            nc.vector.tensor_tensor(tok[:, t, :], tok[:, t, :], tok[:, t, :], ALU.mult)\
                                .then_inc(up_sq, 1)
                        if kind == "res":
                            if i == 0:
                                dve.wait_ge(x_reloaded, 16)
                            xr = x_res[:, t, CW * (i % 2):CW * (i % 2 + 1)]
                            nc.vector.tensor_tensor(xr, acc_of(c, t), xr, ALU.add).then_inc(added, 1)
                    if kind in ("q", "k"):
                        j = QK.index((kind, i))
                        dve.wait_ge(qk_reduced, 2 * j + 2)
                        nc.vector.tensor_scalar(qk_ss[:, :], qk_ss[:, :], 1.0 / HD, EPS, ALU.mult, ALU.add)\
                            .then_inc(qk_sum, 1)
                    if kind == "pc":
                        for t in range(NT):
                            dve.wait_ge(branch, 4 + 2 * i + t + 1)
                            gt = gates[:, t, CW * i:CW * (i + 1)]
                            nc.vector.tensor_tensor(gt, gt, gates[:, t, D + CW * i:D + CW * (i + 1)], ALU.add)\
                                .then_inc(branch_sum, 1)
                if s + LEAD < NU and s not in NORMS and not on_pool(s + LEAD):
                    split_low(s + LEAD)
                for _ in range(max(0, min(quota[s] - 2, 5))):
                    conv_step(taps_done)
                    taps_done += 1
                for g in range(2):
                    if s == ATT[8 * g + 7] + 4:
                        dve.wait_ge(a_pow, g + 1)
                        for qb in range(2):
                            at_ = a_tok[:, qb, CW * g:CW * (g + 1)].rearrange("p (a b) -> p a b", b=P)
                            rr = a_r[:, 8 * g:8 * g + 8].rearrange("p (a b) -> p b a", b=2)[:, qb, :]
                            nc.vector.tensor_tensor(at_, at_, spread(rr, P), ALU.mult).then_inc(a_scaled, 1)
                for _ in range(max(0, quota[s] - 7)):
                    conv_step(taps_done)
                    taps_done += 1
                if s in ended and ended[s][0] in ("q", "k"):
                    kind, i, c = ended[s]
                    j = QK.index((kind, i))
                    dve.wait_ge(qk_pow, j + 1)
                    for t in range(NT):
                        nc.vector.tensor_scalar(qk_c[:, 8 * t:8 * t + 8], qk_r[:, 8 * t:8 * t + 8],
                                                rstd[:, blk, t:t + 1], None, ALU.mult).then_inc(qk_coef, 1)
                    for t in range(NT):
                        dve.wait_ge(qk_coef, 2 * j + t + 1)
                        nc.vector.tensor_tensor(tok[:, t, :].rearrange("p (a b) -> p a b", b=HD),
                                                acc_of(c, t).rearrange("p (a b) -> p a b", b=HD),
                                                spread(qk_c[:, 8 * t:8 * t + 8], HD), ALU.mult).then_inc(qk_normed, 1)
                if s == end["pc", 1]:
                    for g in (2, 3):
                        pair_low(y_hi, y_lo, g, STAGE[g], mix_hi, g + 1, mix_lo)
                if s == end["res", 4]:
                    stage_low(3, 0)
                    stage_low(3, 1)
                for i in (1, 3, 5):
                    if s == end["res", i]:
                        stage_low(i // 2 + 1, 2)
                        stage_low(i // 2 + 1, 3)
                        split_low(s + LEAD)
                        mean_square(i // 2 + 1)
                if s == LN:
                    for i in (0, 1):
                        dve.wait_ge(gate_kept, 2 * i + 2)
                        dve.wait_ge(gate_bias_in[i // 2], 16)
                        gt = gates[:, :, CW * i:CW * (i + 1)]
                        gb = (gate_bias, gate_bias_2)[i // 2][:, i % 2, :]
                        nc.vector.tensor_tensor(gt, gt, again(gb, NT), ALU.add).then_inc(gate_biased, 1)
                if s == LN + 1:
                    dve.wait_ge(ln_sum, 1)
                    for hf in range(2):
                        ch = conv[:, 4 * hf:4 * hf + 4, :]
                        nc.vector.tensor_tensor(ch, ch, again(aux[:, 2, 0:S], 4), ALU.subtract).then_inc(ln_centered, 1)
                    dve.wait_ge(ln_sq, 2)
                    nc.vector.tensor_tensor(centered_sq[:, 0:4, :], centered_sq[:, 0:4, :], centered_sq[:, 4:8, :], ALU.add)\
                        .then_inc(sq_added, 1)
                if s == LN + 2:
                    dve.wait_ge(ln_sum, 2)
                    nc.vector.tensor_scalar(ln_r[:, :], aux[:, 2, 0:S], EPS, None, ALU.add).then_inc(ln_var, 1)
                    dve.wait_ge(ln_sd, 1)
                    nc.vector.reciprocal(ln_r[:, :], ln_r[:, :]).then_inc(ln_rec, 1)
                    dve.wait_ge(ln_rec, 1)
                    for hf in range(2):
                        ch = conv[:, 4 * hf:4 * hf + 4, :]
                        nc.vector.tensor_tensor(ch, ch, again(ln_r[:, :], 4), ALU.mult).then_inc(ln_y, 1)
                    for hf in range(2):
                        dve.wait_ge(conv_hi_ready, hf + 1)
                        nc.vector.tensor_tensor(h_lo[:, 4 * hf:4 * hf + 4, :], conv[:, 4 * hf:4 * hf + 4, :],
                                                f(h_hi[:, 4 * hf:4 * hf + 4, :]), ALU.subtract).then_inc(conv_lo_ready, 1)
                if s == LN + 2:
                    for i in (2, 3):
                        dve.wait_ge(gate_kept, 2 * i + 2)
                        dve.wait_ge(gate_bias_in[i // 2], 16)
                        gt = gates[:, :, CW * i:CW * (i + 1)]
                        gb = (gate_bias, gate_bias_2)[i // 2][:, i % 2, :]
                        nc.vector.tensor_tensor(gt, gt, again(gb, NT), ALU.add).then_inc(gate_biased, 1)
                if s == begin["res", 2]:
                    steps = [0]

                    def link(ins):
                        steps[0] += 1
                        ins.then_inc(sp_dve, 1)
                        dve.wait_ge(sp_dve, steps[0])

                    lam_c, e, den, z, z2, p_ = (vec_t[:, 0:CT2, R_LAMBDA], *(sp_a[:, k, :] for k in (1, 2, 3, 4, 5)))
                    dve.wait_ge(sp_act, 2)
                    link(nc.vector.tensor_scalar(den, e, 2.0, None, ALU.add))
                    link(nc.vector.reciprocal(den, den))
                    link(nc.vector.tensor_tensor(z, e, den, ALU.mult))
                    link(nc.vector.tensor_tensor(z2, z, z, ALU.mult))
                    link(nc.vector.tensor_scalar(p_, z2, 1.0 / 15, None, ALU.mult))
                    for k in (13, 11, 9, 7, 5, 3):
                        link(nc.vector.scalar_tensor_tensor(out=p_, in0=p_, scalar=1.0 / k, in1=z2, op0=ALU.add,
                                                            op1=ALU.mult))
                    link(nc.vector.scalar_tensor_tensor(out=p_, in0=p_, scalar=1.0, in1=z, op0=ALU.add, op1=ALU.mult))
                    link(nc.vector.tensor_scalar(den, lam_c, -1.0, 0.0, ALU.mult, ALU.max))
                    link(nc.vector.scalar_tensor_tensor(out=p_, in0=p_, scalar=2.0, in1=den, op0=ALU.mult, op1=ALU.add))
                    nc.vector.tensor_scalar(coef[:, :], p_, -LRU_C, None, ALU.mult).then_inc(coef_ready, 1)
                if s in (B + 3, B + 4):
                    dve.wait_ge(x2_in, 2)
                    dve.wait_ge(pads_ready, 1)
                    for tap in range(2 * (s - B - 3), 2 * (s - B - 3) + 2):
                        for ct in range(CT2):
                            if tap == 0:
                                nc.vector.tensor_scalar(lru_u[:, ct, :], x2_t[:, ct, 0:S], vcol(R_CONV2_W, ct),
                                                        vcol(R_CONV2_B, ct), ALU.mult, ALU.add).then_inc(u2_ready, 1)
                            else:
                                dve.wait_ge(u2_ready, CT2 * (tap - 1) + ct + 1)
                                nc.vector.scalar_tensor_tensor(out=lru_u[:, ct, :], in0=x2_t[:, ct, tap:tap + S],
                                                               scalar=vcol(R_CONV2_W + tap, ct), in1=lru_u[:, ct, :],
                                                               op0=ALU.mult, op1=ALU.add).then_inc(u2_ready, 1)
                if s == B + 6:
                    dve.wait_ge(ri_kept, 2 * CT2)
                    nc.vector.tensor_tensor(in_gate[:, :, :], in_gate[:, :, :], lru_u[:, :, :], ALU.mult).then_inc(iu_ready, 1)
                    dve.wait_ge(lru_act, 2 * CT2)
                    nc.vector.tensor_tensor(decay_gate[:, :, :], decay[:, :, :], decay[:, :, :], ALU.mult).then_inc(lru_dve, 1)
                    dve.wait_ge(lru_dve, 1)
                    nc.vector.scalar_tensor_tensor(out=lru_tmp[:, :, :], in0=decay_gate[:, :, :], scalar=1.0, in1=lru_tmp[:, :, :],
                                                   op0=ALU.add, op1=ALU.mult).then_inc(lru_dve, 1)
                if s == B + 8:
                    dve.wait_ge(lru_root, 1)
                    dve.wait_ge(iu_ready, 1)
                    nc.vector.tensor_tensor(in_gate[:, :, :], in_gate[:, :, :], lru_tmp[:, :, :], ALU.mult).then_inc(lru_dve, 1)
                    dve.wait_ge(lru_dve, 3)
                    for ct in range(CT2):
                        nc.vector.tensor_tensor_scan(lru_u[:, ct, :], decay[:, ct, :], in_gate[:, ct, :], 0.0, ALU.mult, ALU.add)\
                            .then_inc(lru_dve, 1)
                    softplus_sum(0)
                if s == B + 9:
                    dve.wait_ge(lru_dve, 3 + CT2)
                    dve.wait_ge(g2_in, 2)
                    nc.vector.tensor_tensor(lru_tmp[:, :, :], lru_u[:, :, :], gelu_t[:, :, :], ALU.mult).then_inc(lru_out, 1)
                    softplus_sum(1)
                    log_weights(0)
                    dve.wait_ge(lru_hi, 1)
                    nc.vector.tensor_tensor(y_lo[:, CT2:KT, :], lru_tmp[:, :, :], f(y_hi[:, CT2:KT, :]), ALU.subtract)\
                        .then_inc(lru_lo, 1)
                if s == B + 10:
                    log_weights(1)
                    softplus_sum(2)
                    softplus_sum(3)
                if s == B + 11:
                    log_weights(2)
                    log_weights(3)
                    for n in range(4):
                        pv2_low(n)

        @block.tensor
        def _(pe):
            held = {}

            def claim(places, sem_, value):
                for p_ in places:
                    if p_ in held:
                        pe.wait_ge(*held[p_])
                    held[p_] = (sem_, value)

            def turn(out_, in_):
                return nc.tensor.transpose(out_, in_, ident[:, :])

            def turn_pair(src, g, bank):
                for j in range(2):
                    for t in range(NT):
                        kt = 2 * g + j
                        mm = turn(aux[:, bank, 256 * j + P * t:256 * j + P * (t + 1)], src[:, t, P * kt:P * (kt + 1)])
                return mm

            def turn_four(src, dst=aux[:, 2, :]):
                for k in range(4):
                    mm = turn(dst[:, P * k:P * (k + 1)], src[:, P * k:P * (k + 1)])
                return mm

            def stage(st, pairs):
                src = x_res if st else x_in
                for g in pairs:
                    claim([STAGE[g]], stage_lo, 8 * st + 2 * g + 2)
                    turn_pair(src, g, STAGE[g]).then_inc(stage_turned, 1)

            def turn_glu(i, t):
                pe.wait_ge(glu_made, 2 * i + t + 1)
                claim([2], glu_kept, 2 * i + t + 1)
                for j in range(2):
                    mm = turn(aux[:, 2, P * j:P * (j + 1)], glu[:, t, P * j:P * (j + 1)])
                mm.then_inc(glu_turned, 1)

            def turn_qk(kind, i, t):
                j = QK.index((kind, i))
                pe.wait_ge(qk_normed, 2 * j + t + 1)
                claim([2], qk_kept, 2 * j + t + 1)
                turn_four(tok[:, t, :]).then_inc(qk_turned, 1)

            def scores(n):
                hd, qb = n // 2, n % 2
                if n in (0, 8):
                    pe.wait_ge(qk_kept, 4 * (n // 8) + 4)
                claim([0, 1], biased, n + 1)
                for m in range(2):
                    ps = slice(HD * m, HD * (m + 1))
                    mm = nc.tensor.matmul(aux[:, m, 0:P * (qb + 1)], q_t[ps, hd, P * qb:P * (qb + 1)],
                                          k_t[ps, hd, 0:P * (qb + 1)], start=True, stop=True)
                mm.then_inc(scored, 1)

            def turn_probs(n):
                pe.wait_ge(mixed, n + 1)
                claim([3], probs_kept, n + 1)
                for k in range(n % 2 + 1):
                    mm = turn(aux[:, 3, P * k:P * (k + 1)], probs[:, n % 2, 0, P * k:P * (k + 1)])
                mm.then_inc(probs_turned, 1)

            def attend(n):
                hd, qb = n // 2, n % 2
                pe.wait_ge(probs_kept, n + 1)
                pe.wait_ge(v_kept, 2 * (hd // 4) + 2)
                claim([3], a_kept, n + 1)
                for k in range(qb + 1):
                    mm = nc.tensor.matmul(aux[:, 3, 0:P], probs_t[:, n % 2, k, :],
                                          v_tok[:, k, P * hd:P * (hd + 1)], start=(k == 0), stop=(k == qb))
                mm.then_inc(pv_done, 1)

            def channel_sum(src, n):
                claim([2], *((ln_centered, 2) if n == 0 else (ln_var, 1)))
                kts = (0, 6, 7) if n == 0 else range(4)
                for kt in kts:
                    moving = conv_sum[:, :] if n == 0 and kt == 0 else src[:, kt, :]
                    mm = nc.tensor.matmul(aux[:, 2, 0:S], mean_w[:, :], moving, start=(kt == 0), stop=(kt == kts[-1]))
                mm.then_inc(ln_sum, 1)

            def scores2(n):
                if n == 0:
                    pe.wait_ge(qk_kept, 12)
                for j in range(2):
                    bank = 2 * (n % 2) + j
                    claim([bank], lw_ready, n + 1)
                    ps = slice(HD * j, HD * (j + 1))
                    nc.tensor.matmul(aux[:, bank, 0:S], k2_t[ps, n, 0:P], q2_t[ps, n, 0:S], start=True, stop=False,
                                     skip_group_check=True)
                    mm = nc.tensor.matmul(aux[:, bank, S:ZC], k2_t[ps, n, P:S], q2_t[ps, n, P:S], start=False,
                                          stop=False, skip_group_check=True)
                mm.then_inc(z_made, 1)

            def suffixes(n):
                pe.wait_ge(sp_ready, n + 1)
                for j in range(2):
                    bank, sp_ = 2 * (n % 2) + j, w2_t[:, 2 * n + j, :]
                    nc.tensor.matmul(aux[:, bank, 0:S], neg_tri[:, :], sp_[:, 0:S], start=False, stop=False,
                                     skip_group_check=True)
                    nc.tensor.matmul(aux[:, bank, P:S], neg_one[:, :], sp_[:, S:ZC], start=False, stop=False,
                                     skip_group_check=True)
                    mm = nc.tensor.matmul(aux[:, bank, S:ZC], neg_tri[:, :], sp_[:, S:ZC], start=False, stop=True,
                                          skip_group_check=True)
                mm.then_inc(sfx_done, 1)

            def attend2(n):
                pe.wait_ge(w2_ready, n + 1)
                claim([n], o2_lo, n + 1)
                for j in range(2):
                    ps = slice(HD * j, HD * (j + 1))
                    c0 = HD * (2 * n + j)
                    nc.tensor.matmul(aux[ps, n, 0:S], v2[:, 0, c0:c0 + HD], w2_t[:, 2 * n + j, 0:S], start=True,
                                     stop=False, skip_group_check=True)
                    mm = nc.tensor.matmul(aux[ps, n, P:S], v2[:, 1, c0:c0 + HD], w2_t[:, 2 * n + j, S:ZC],
                                          start=False, stop=True, skip_group_check=True)
                mm.then_inc(pv2_done, 1)

            def lru_gates(ct):
                pe.wait_ge(u2_ready, TAPS2 * CT2)
                pe.wait_ge(lru_w_in, 64)
                bank = LRU_BANK[ct]
                claim([bank], ri_kept, 2 * ct + 2)
                nc.tensor.matmul(aux[:, bank, 0:S], wr_g[:, ct, :], lru_u[:, ct, :], start=True, stop=True)
                nc.tensor.matmul(aux[:, bank, S:2 * S], wi_g[:, ct, :], lru_u[:, ct, :], start=True, stop=True)\
                    .then_inc(ri_made, 1)

            def wait_stationary(c, k1):
                kind, i = chunks[c][:2]
                if kind == "pc":
                    pe.wait_ge(conv_lo_ready, k1 // 4)
                elif kind == "pa":
                    pe.wait_ge(a_lo, k1 // 2)
                elif kind == "res" and i < 2:
                    pe.wait_ge(mix_lo, k1 // 2)
                elif kind == "res" and i < 4:
                    pe.wait_ge(ff_lo, k1 // 2)
                elif kind == "res" and i < 6:
                    if k1 > CT2:
                        pe.wait_ge(lru_lo, 1)
                    else:
                        pe.wait_ge(o2_lo, 4)
                elif kind == "res":
                    pe.wait_ge(up_lo, k1 // 2)
                else:
                    st = {"ff": 1, "up": 3}.get(kind, 0 if c <= number["g", 3] else 2)
                    pe.wait_ge(stage_lo, 8 * st + k1)

            def parts(c):
                kind, i = chunks[c][:2]
                if kind == "pa" or (kind == "res" and i in (0, 1, 4, 5)):
                    return y_hi, y_lo
                if kind == "res":
                    return m_hi, m_lo
                return h_hi, h_lo

            def halfway(s):
                for i in range(4):
                    if s == end["u", i] + 1:
                        turn_glu(i, 0)
                for kind, i in QK:
                    if i < 2 and s == end[kind, i] + 2:
                        turn_qk(kind, i, 1)
                    if i == 2 and s == end[kind, i] + 1:
                        turn_qk(kind, i, 0)
                for n in range(NA):
                    if s == ATT[n] + 3:
                        attend(n)
                if s == end["pc", 1]:
                    turn_mix((2, 3))
                if s == end["res", 4]:
                    pe.wait_ge(added, 10)
                    stage(3, (0, 1))
                for i in (1, 3, 5):
                    if s == end["res", i]:
                        pe.wait_ge(added, 2 * i + 2)
                        stage(i // 2 + 1, (2, 3))
                if s == B + 3:
                    turn2(x2_tok, 1, x2_kept, x2_turned, x2_in)
                if s == B + 6:
                    lru_gates(3)
                if s == B + 8:
                    scores2(0)
                if s == B + 9:
                    suffixes(0)
                if s == B + 10:
                    scores2(3)
                if s == B + 11:
                    suffixes(3)
                    pe.wait_ge(v_kept, 6)
                    attend2(0)
                    attend2(1)

            def turn_mix(pairs):
                pe.wait_ge(branch_sum, 2 * (pairs[0] // 2) + 2)
                for g in pairs:
                    claim([STAGE[g]], mix_lo, g + 1)
                    turn_pair(gates, g, STAGE[g]).then_inc(mix_turned, 1)

            def turn2(src, t, s_in, s_out, s_kept):
                pe.wait_ge(s_in, t + 1)
                if src is g2_tok:
                    turn_four(src[:, t, :], acc_of(number["g2", 0], t)).then_inc(s_out, 1)
                    return
                claim([2], s_kept, t + 1)
                turn_four(src[:, t, :]).then_inc(s_out, 1)

            def after(s):
                if s == 0:
                    pe.wait_ge(consts_loaded, 32)
                    pe.wait_ge(zeros_ready, 5)
                    claim([2], rel_kept, 1)
                    nc.tensor.matmul(aux[0:H, 2, 0:RELS], rel_aug[:, :], onehot[:, :], start=True, stop=True)\
                        .then_inc(rel_made, 1)
                for i in range(4):
                    if s == end["u", i] + 1:
                        turn_glu(i, 1)
                for kind, i in QK:
                    if s == end[kind, i] + 1:
                        turn_qk(kind, i, 0 if i < 2 else 1)
                for n in range(NA):
                    if s == ATT[n] + 2:
                        turn_probs(n)
                for n in range(NA):
                    if s == ATT[n]:
                        scores(n)
                if s == LN:
                    pe.wait_ge(conv_done, CONV_OPS)
                    pe.wait_ge(conv_added, 5)
                    channel_sum(conv, 0)
                if s == LN + 1:
                    pe.wait_ge(sq_added, 1)
                    channel_sum(centered_sq, 1)
                if s in a_steps:
                    for g in a_steps[s]:
                        pe.wait_ge(a_scaled, 2 * (g // 2) + 2)
                        claim([g % 2], a_lo, g + 1)
                        turn_pair(a_tok, g, g % 2).then_inc(a_turned, 1)
                if s == end["pc", 0]:
                    turn_mix((0, 1))
                for i in (0, 2):
                    if s == end["res", i]:
                        pe.wait_ge(added, 2 * i + 2)
                        stage(i // 2 + 1, (0, 1))
                for i in range(FF // 256):
                    if s == end["ff", i]:
                        pe.wait_ge(ff_made, 2 * i + 2)
                        claim([i % 2], ff_lo, i + 1)
                        for j in range(2):
                            for t in range(NT):
                                mm = turn(aux[:, i % 2, 256 * j + P * t:256 * j + P * (t + 1)],
                                          ff_m[:, t, P * j:P * (j + 1)])
                        mm.then_inc(ff_turned, 1)
                for i in range(FF2 // CW):
                    if s == end["up", i]:
                        pe.wait_ge(up_sq, 2 * i + 2)
                        for j in range(2):
                            claim([j], up_lo, 2 * i + j + 1)
                            turn_pair(tok, j, j).then_inc(up_turned, 1)
                if s == B + 2:
                    turn2(x2_tok, 0, x2_kept, x2_turned, x2_in)
                if s == B + 5:
                    for ct in range(3):
                        lru_gates(ct)
                if s == B + 8:
                    scores2(1)
                    turn2(g2_tok, 0, g2_kept, g2_turned, g2_in)
                    turn2(g2_tok, 1, g2_kept, g2_turned, g2_in)
                if s == B + 9:
                    suffixes(1)
                    scores2(2)
                if s == B + 10:
                    suffixes(2)
                if s == B + 11:
                    attend2(2)
                    attend2(3)

            pe.wait_ge(ident_ready, 1)
            pe.wait_ge(vecs_loaded, 16)
            claim([2], vec_ready, 1)
            for kt in range(KT):
                mm = nc.tensor.transpose(aux[:, 2, VROWS * kt:VROWS * (kt + 1)], vecs[:, P * kt:P * (kt + 1)],
                                         ident[0:VROWS, 0:VROWS])
            mm.then_inc(vec_turned, 1)
            for t in range(NT):
                pe.wait_ge(x_loaded[t], 16)
            stage(0, range(4))
            for s, (c, k0, nk, is_first, is_last) in enumerate(units):
                if is_first and c >= 2:
                    pe.wait_ge(*freed_by(c - 2))
                wait_stationary(c, k0 + nk)
                pe.wait_ge(w_hi_ready, s + 1)
                pe.wait_ge(w_lo_pool if on_pool(s) else w_lo_dve, low_no[s])
                hi, lo = parts(c)
                slot = s % SPLIT
                for j in range(nk):
                    for t in range(NT):
                        o = acc_of(c, t)
                        x_h = hi[:, k0 + j, P * t:P * (t + 1)]
                        x_l = lo[:, k0 + j, P * t:P * (t + 1)]
                        begin_ = is_first and j == 0
                        end_ = is_last and j == nk - 1
                        nc.tensor.matmul(o, x_h, w_hi[:, slot, j, :], start=begin_, stop=False)
                        nc.tensor.matmul(o, x_h, w_lo[:, slot, j, :], start=False, stop=False)
                        mm = nc.tensor.matmul(o, x_l, w_hi[:, slot, j, :], start=False, stop=end_)
                    if j == nk - 1:
                        mm.then_inc(unit_done, 1)
                    if j == 1:
                        halfway(s)
                after(s)


def t5_one_hot():
    e = np.zeros((VROWS, RELS), np.float32)
    exact = BUCKETS // 2
    for m in range(RELS):
        n = 255 - m
        if n < 0:
            e[BUCKETS, m] = 1.0
            continue
        b = n
        if n >= exact:
            b = min(exact + int(math.log(n / exact) / math.log(MAX_DIST / exact) * (BUCKETS - exact)), BUCKETS - 1)
        e[b, m] = 1.0
    return e


def small_vectors(g):
    v = np.zeros((VROWS, D), np.float32)
    rows = [(R_CONV_W, g["conv_w"][0]), (R_CONV_B, g["conv_b"]), (R_LN_W, g["conv_ln_w"]), (R_LN_B, g["conv_ln_b"]),
            (R_NORM[0], g["attn_norm_w"]), (R_NORM[1], g["ffn_norm_w"]), (R_NORM[2], g["norm1_g_2"]),
            (R_NORM[3], g["norm2_g_2"]), (R_CONV2_W, g["conv_w_2"][0]), (R_CONV2_B, g["conv_b_2"]),
            (R_RG, g["b_rg_2"]), (R_IG, g["b_ig_2"]), (R_LAMBDA, g["lru_lambda_2"]),
            (R_Q, np.concatenate([g["q_norm_w"]] * 2, 1)), (R_K, np.concatenate([g["k_norm_w"]] * 2, 1)),
            (R_SUB, g["subln_w"]), (R_Q2, np.concatenate([g["q_norm_g_2"]] * 2, 1)),
            (R_K2, np.concatenate([g["k_norm_g_2"]] * 2, 1))]
    for r, x in rows:
        v[r:r + x.shape[0], 0:x.shape[1]] = x
    return v


DIRECT = ["x", "lam_q1", "lam_k1", "lam_q2", "lam_k2", "gate_b", "rel_bias", "w_in", "w_proj_attn", "w_proj_conv",
          "w_out", "w_gate_up", "w_down", "w_in_2", "w_rg_2", "w_ig_2", "w_out_2", "w_up_2", "w_down_2"]
WEIGHTS = ["w_in", "w_proj_attn", "w_proj_conv", "w_out", "w_gate_up", "w_down", "w_in_2", "w_out_2", "w_up_2",
           "w_down_2"]


def kernel(**inputs):
    import concourse.bacc as bacc
    from concourse.bass_utils import run_bass_kernel_spmd

    g = {k: np.ascontiguousarray(v) for k, v in inputs.items()}
    arrays = {f"{k}_dram": g[k] for k in DIRECT}
    arrays["vectors_dram"] = small_vectors(g)
    arrays["bucket_onehot_dram"] = t5_one_hot()
    nc = bacc.Bacc("TRN2", target_bir_lowering=False, num_devices=1)
    aps = {k[:-5]: nc.dram_tensor(k, v.shape, F32, kind="ExternalInput").ap() for k, v in arrays.items()}
    for k in WEIGHTS:
        aps[k] = aps[k].rearrange("o k n -> (o k) n")
    out = nc.dram_tensor("out_dram", (1, S, D), F32, kind="ExternalOutput").ap()
    build(nc, aps, out)
    r = run_bass_kernel_spmd(nc, [arrays], core_ids=[0])
    return r.results[0]["out_dram"]
```
